# Optimizing a Trainium2 kernel written in Bass

```python
import jax, jax.numpy as jnp
from jax import lax
import numpy as np

D_MODEL = 1024
BATCH = 1
SEQ = 256
DEPTH = 2

CTX_LEN = 256
GRID_W = 64
GLA_HEADS = 4
GLA_DK = 64
GLA_DV = 128
GLA_KW = GLA_HEADS * GLA_DK
GLA_VW = GLA_HEADS * GLA_DV
DECAY_RANK = 16
GATE_NORMALIZER = 16.0
CHUNK = 64
CONV_CH = D_MODEL - GLA_VW
CONV_K = 3
MIX_W = GLA_VW + CONV_CH
PROJ_SIZES = (GLA_KW, GLA_KW, GLA_VW, GLA_VW, DECAY_RANK, DECAY_RANK, CONV_CH, CONV_CH, CONV_CH)
PROJ_W = sum(PROJ_SIZES)
D_FF = 2816
N_EXPERTS = 8
TOP_K = 2
D_FF_EXPERT = 3584
N_DENSE = (DEPTH + 1) // 2
N_MOE = DEPTH // 2
EPS = 1e-6

kernel_name = "hybrid_gla_shortconv_moe_dit"

def rmsnorm(x, g):
    xf = x.astype(jnp.float32)
    y = xf * lax.rsqrt(jnp.mean(xf * xf, axis=-1, keepdims=True) + EPS)
    return (y * g.astype(jnp.float32)).astype(x.dtype)

def modulate(x, shift, scale):
    return x * (1 + scale) + shift

def split_proj(p):
    idx = [int(v) for v in np.cumsum(PROJ_SIZES)[:-1]]
    return jnp.split(p, idx, axis=-1)

def to_heads(t, dh):
    b, l, w = t.shape
    return t.reshape(b, l, w // dh, dh).transpose(0, 2, 1, 3)

def gla_chunk_scan(q, k, v, log_a, s0):
    b_, h_, l_, dk = q.shape
    dv = v.shape[-1]
    nc = l_ // CHUNK

    def to_chunks(t):
        return t.reshape(b_, h_, nc, CHUNK, t.shape[-1]).transpose(2, 0, 1, 3, 4)

    tril = jnp.tril(jnp.ones((CHUNK, CHUNK), dtype=bool))

    def step(s, inp):
        qc, kc, vc, gc = [t.astype(jnp.float32) for t in inp]
        bcum = jnp.cumsum(gc, axis=-2)
        o_inter = jnp.einsum('bhcd,bhde->bhce', qc * jnp.exp(bcum), s)
        diff = bcum[:, :, :, None, :] - bcum[:, :, None, :, :]
        decay = jnp.exp(jnp.where(tril[:, :, None], diff, -jnp.inf))
        attn = jnp.einsum('bhid,bhijd->bhij', qc, decay * kc[:, :, None, :, :])
        o_intra = jnp.einsum('bhij,bhje->bhie', attn, vc)
        b_last = bcum[:, :, -1, :]
        s_new = jnp.exp(b_last)[..., None] * s + jnp.einsum(
            'bhjd,bhje->bhde', kc * jnp.exp(b_last[:, :, None, :] - bcum), vc)
        return s_new, o_inter + o_intra

    s_fin, o = lax.scan(step, s0, (to_chunks(q), to_chunks(k), to_chunks(v), to_chunks(log_a)))
    o = o.transpose(1, 2, 0, 3, 4).reshape(b_, h_, l_, dv)
    return o.astype(q.dtype), s_fin

def gla_bidir(q, k, v, la_f, la_b, s0_f, s0_b):
    o_f, s_f = gla_chunk_scan(q, k, v, la_f, s0_f)
    flip = lambda t: jnp.flip(t, axis=2)
    o_b, s_b = gla_chunk_scan(flip(q), flip(k), flip(v), flip(la_b), s0_b)
    return o_f + flip(o_b), s_f, s_b

def gla_inputs(parts, w_dec, b_dec):
    q, k, v, _, a_f, a_b = parts[:6]
    qh = to_heads(q * (GLA_DK ** -0.5), GLA_DK)
    kh = to_heads(k, GLA_DK)
    vh = to_heads(v, GLA_DV)
    la_f = to_heads(jax.nn.log_sigmoid(a_f @ w_dec[0] + b_dec[0]) / GATE_NORMALIZER, GLA_DK)
    la_b = to_heads(jax.nn.log_sigmoid(a_b @ w_dec[1] + b_dec[1]) / GATE_NORMALIZER, GLA_DK)
    return qh, kh, vh, la_f, la_b

def gla_output(o, g, gain):
    b_, h_, l_, dv = o.shape
    on = rmsnorm(o, gain).transpose(0, 2, 1, 3).reshape(b_, l_, h_ * dv)
    return on * jax.nn.silu(g)

def short_conv(gate_b, gate_c, h, w, n_seg, seg_len):
    b_, l_, ch = h.shape
    u = (gate_c * h).reshape(b_ * n_seg, seg_len, ch)
    y = lax.conv_general_dilated(u, w[:, None, :].astype(u.dtype), window_strides=(1,), padding='SAME',
                                 dimension_numbers=('NWC', 'WIO', 'NWC'), feature_group_count=ch)
    return gate_b * y.reshape(b_, l_, ch)

def swiglu(h, w1, w3, w2):
    return (jax.nn.silu(h @ w1) * (h @ w3)) @ w2

def moe_swiglu(h, w_r, w1e, w3e, w2e):
    logits = (h @ w_r).astype(jnp.float32)
    vals, idx = lax.top_k(logits, TOP_K)
    wts = jax.nn.softmax(vals, axis=-1)
    comb = jnp.sum(jax.nn.one_hot(idx, N_EXPERTS, dtype=jnp.float32) * wts[..., None], axis=-2).astype(h.dtype)
    out = jnp.zeros_like(h)
    for e in range(N_EXPERTS):
        out = out + comb[..., e:e + 1] * swiglu(h, w1e[e], w3e[e], w2e[e])
    return out

def setup_inputs(seed: int = 0) -> dict:
    key = jax.random.key(seed)
    ks = iter(jax.random.split(key, 32))
    nrm = lambda shape, scale: jax.random.normal(next(ks), shape, jnp.float32) * scale
    gain = lambda shape: 1.0 + nrm(shape, 0.02)
    d = D_MODEL
    return {
        "x": nrm((BATCH, SEQ, d), 1.0),
        "c": nrm((BATCH, d), 1.0),
        "ctx": nrm((BATCH, CTX_LEN, d), 1.0),
        "c_ctx": nrm((d,), 1.0),
        "w_mod": nrm((DEPTH, d, 6 * d), d ** -0.5),
        "b_mod": nrm((DEPTH, 6 * d), 0.02),
        "g_mix_pre": gain((DEPTH, d)),
        "g_mix_post": gain((DEPTH, d)),
        "w_in": nrm((DEPTH, d, PROJ_W), d ** -0.5),
        "w_decay": nrm((DEPTH, 2, DECAY_RANK, GLA_KW), DECAY_RANK ** -0.5),
        "b_decay": nrm((DEPTH, 2, GLA_KW), 0.5),
        "gla_norm": gain((DEPTH, GLA_DV)),
        "conv_w": nrm((DEPTH, CONV_K, CONV_CH), CONV_K ** -0.5),
        "w_out": nrm((DEPTH, MIX_W, d), MIX_W ** -0.5),
        "g_ffn_pre": gain((DEPTH, d)),
        "g_ffn_post": gain((DEPTH, d)),
        "w1": nrm((N_DENSE, d, D_FF), d ** -0.5),
        "w3": nrm((N_DENSE, d, D_FF), d ** -0.5),
        "w2": nrm((N_DENSE, D_FF, d), D_FF ** -0.5),
        "w_router": nrm((N_MOE, d, N_EXPERTS), d ** -0.5),
        "e_w1": nrm((N_MOE, N_EXPERTS, d, D_FF_EXPERT), d ** -0.5),
        "e_w3": nrm((N_MOE, N_EXPERTS, d, D_FF_EXPERT), d ** -0.5),
        "e_w2": nrm((N_MOE, N_EXPERTS, D_FF_EXPERT, d), D_FF_EXPERT ** -0.5),
    }

def reference(x, c, ctx, c_ctx, w_mod, b_mod, g_mix_pre, g_mix_post, w_in, w_decay, b_decay, gla_norm,
              conv_w, w_out, g_ffn_pre, g_ffn_post, w1, w3, w2, w_router, e_w1, e_w3, e_w2):
    b_, l_, _ = x.shape
    rows = l_ // GRID_W
    ctx_len = ctx.shape[1]
    silu_c = jax.nn.silu(c)
    silu_cc = jax.nn.silu(c_ctx)
    xc = ctx
    for i in range(DEPTH):
        last = i == DEPTH - 1
        sh1, sc1, gt1, sh2, sc2, gt2 = jnp.split((silu_c @ w_mod[i] + b_mod[i])[:, None, :], 6, axis=-1)
        csh1, csc1, cgt1, csh2, csc2, cgt2 = jnp.split(silu_cc @ w_mod[i] + b_mod[i], 6, axis=-1)

        p = split_proj(modulate(rmsnorm(x, g_mix_pre[i]), sh1, sc1) @ w_in[i])
        pc = split_proj(modulate(rmsnorm(xc, g_mix_pre[i]), csh1, csc1) @ w_in[i])

        s_zero = jnp.zeros((ctx.shape[0], GLA_HEADS, GLA_DK, GLA_DV), jnp.float32)
        o_c, s_f, s_b = gla_bidir(*gla_inputs(pc, w_decay[i], b_decay[i]), s_zero, s_zero)
        o_x, _, _ = gla_bidir(*gla_inputs(p, w_decay[i], b_decay[i]), s_f, s_b)

        y_x = jnp.concatenate([
            gla_output(o_x, p[3], gla_norm[i]),
            short_conv(p[6], p[7], p[8], conv_w[i], rows, GRID_W),
        ], axis=-1) @ w_out[i]
        x = x + gt1 * rmsnorm(y_x, g_mix_post[i])
        if not last:
            y_c = jnp.concatenate([
                gla_output(o_c, pc[3], gla_norm[i]),
                short_conv(pc[6], pc[7], pc[8], conv_w[i], 1, ctx_len),
            ], axis=-1) @ w_out[i]
            xc = xc + cgt1 * rmsnorm(y_c, g_mix_post[i])

        j = i // 2
        if i % 2 == 0:
            ffn = lambda h: swiglu(h, w1[j], w3[j], w2[j])
        else:
            ffn = lambda h: moe_swiglu(h, w_router[j], e_w1[j], e_w3[j], e_w2[j])
        x = x + gt2 * rmsnorm(ffn(modulate(rmsnorm(x, g_ffn_pre[i]), sh2, sc2)), g_ffn_post[i])
        if not last:
            xc = xc + cgt2 * rmsnorm(ffn(modulate(rmsnorm(xc, g_ffn_pre[i]), csh2, csc2)), g_ffn_post[i])
    return x


_drawn_inputs = setup_inputs


def setup_inputs(seed=0):
    import zlib

    import numpy as np

    out = dict(_drawn_inputs(seed))
    spreads = {}
    factors = {'gla_norm': 4.047}
    for name, (base, spread) in spreads.items():
        noise = np.random.default_rng([zlib.crc32(name.encode()), seed]).standard_normal(out[name].shape)
        drawn = base * np.exp(spread * noise) if base else spread * noise
        out[name] = __import__('jax').numpy.asarray(drawn.astype(out[name].dtype))
    for name, factor in factors.items():
        out[name] = (out[name] * factor).astype(out[name].dtype)
    return out
```

```python
from contextlib import ExitStack

import numpy as np

import concourse.bass as bass
from concourse import mybir

F32 = mybir.dt.float32
BF16 = mybir.dt.bfloat16
I32 = mybir.dt.int32
U8 = mybir.dt.uint8
ALU = mybir.AluOpType
ACT = mybir.ActivationFunctionType
AX_X = mybir.AxisListType.X

P = 128
D = 1024
KD = D // P
CTX, SEQ = 256, 256
TOK = CTX + SEQ
TT = SEQ // P
DEPTH = 2
HEADS, DK, DV = 4, 64, 128
RT = HEADS * DK // P
RANK = 16
CHUNK = 64
NCH = TOK // CHUNK
NG = TOK // P
GATE_NORM = 16.0
EPS = 1e-6
DFF = 2816
JF = DFF // P
NE = 8
DFE = 3584
JE = DFE // P
LEVELS = [32, 16, 8, 4, 2, 1]
COL = {"qk": 0, "v": 512, "g": 1024, "a": 1536, "B": 1568, "C": 2080, "h": 2592}

BM, GMP, GMO, GFP, GFO, BD, GN, CW, CC, CX = 0, 48, 56, 64, 72, 80, 84, 85, 97, 105
VROWS = 113

SLOTS = 5
CHUNKW = KD * 512
ESLOTS = 7
PIECE = 3 * D
WIDTHS = (64, 128, 256)
BODY = 14
MISC = 14


def by_width(eng, chosen, body):
    with eng.If(chosen > WIDTHS[1]):
        body(WIDTHS[2])
    with eng.If(chosen < WIDTHS[1] + 1):
        with eng.If(chosen > WIDTHS[0]):
            body(WIDTHS[1])
        with eng.If(chosen < WIDTHS[0] + 1):
            body(WIDTHS[0])


def plan():
    uses = []
    turn = [0]

    def use(name, bank, *chunks):
        uses.append((name, bank, chunks))

    def rot():
        turn[0] += 1
        return (turn[0] - 1) % 4

    def mod(layer, s, bank=None):
        use(("mod", layer, s), rot() if bank is None else bank, ("mod", layer, 2 * s), ("mod", layer, 2 * s + 1))

    use(("vec", 0), 6)
    use(("vec", 1), 7)
    for k in range(KD):
        use(("xt", k), rot())
    for s in range(6):
        mod(0, s)
    for L in range(DEPTH):
        blocks = range(4) if L == 0 else range(2, 4)
        use(("ssq", 2 * L), 4)
        for m in range(RT):
            use(("q", L, m), rot(), ("qk", L))
        for m in range(RT):
            use(("k", L, m), rot(), ("qk", L))
        use(("a", L), rot(), ("a", L))
        for i in range(4):
            use(("z", L, i), rot())
        for g in range(NG):
            use(("v", L, g), rot(), ("v", L))
        for b in blocks:
            use(("P", L, 0, b), 4 + b)
        for s in range(len(LEVELS)):
            if s < 2:
                use(("g", L, 2 * s), rot(), ("g", L))
                use(("g", L, 2 * s + 1), rot(), ("g", L))
            else:
                for w in "ChB":
                    use((w, L, s - 2), rot(), (w, L))
            for b in blocks:
                use(("P", L, s + 1, b), 4 + b)
        if L == 0:
            mod(1, 0)
            mod(1, 1)
        for i in range(4):
            use(("kt", L, i), 4 + i)
        if L == 0:
            mod(1, 2)
        for i in range(4):
            use(("U", L, 0, i), rot())
        for i in range(4):
            use(("U", L, 1, i), 4 + i)
        if L == 0:
            mod(1, 3)
            mod(1, 4)
        for h in range(HEADS):
            use(("o", L, h), rot())
        if L == 0:
            mod(1, 5, 7)
        for h in range(HEADS):
            use(("oss", L, h), 4 + h)
        for m in range(KD):
            use(("y", L, m), rot(), ("wo", L, m // 4))
        use(("yss", 2 * L), 4)
        use(("ssq", 2 * L + 1), 5)
        if L == 0:
            for j in range(JF):
                use(("ffg", j), rot(), ("ff", j // 2))
                use(("ffu", j), rot(), ("ff", j // 2))
            for half in range(2):
                for m in range(4):
                    use(("y2", 4 * half + m), 4 + m if half == 0 else rot(), *[("w2", half, i) for i in range(3)])
            use(("yss", 1), 4)
    use(("lg",), 6)
    for i in range(4):
        use(("ht", i), rot())
    use(("pos",), 7)
    use(("yss", 3), 4)
    for i in range(4):
        use(("out", i), rot())
    return uses


def hybrid_backbone(nc, x, c, ctx_in, c_ctx, w_mod, b_mod, g_mix_pre, g_mix_post, w_in, w_decay, b_decay, gla_norm,
                    conv_w, w_out, g_ffn_pre, g_ffn_post, w1, w3, w2, w_router, e_w1, e_w3, e_w2, out):
    uses = plan()
    tile_at, bank_of, nth_of = {}, {}, {}
    chunk_order, chunk_last = [], {}
    count = [0] * 8
    for n, (name, bank, chunks) in enumerate(uses):
        tile_at[name], bank_of[name], nth_of[name] = n, bank, count[bank]
        count[bank] += 1
        for ch in chunks:
            if ch not in chunk_last:
                chunk_order.append(ch)
            chunk_last[ch] = n
    chunk_at = {ch: i for i, ch in enumerate(chunk_order)}
    slot_sum = [0] * SLOTS
    chunk_value = {}
    for i, ch in enumerate(chunk_order):
        slot_sum[i % SLOTS] += 32 if ch[0] == "ff" else 16
        chunk_value[ch] = slot_sum[i % SLOTS]

    sums = [(name, 1 if name[0] == "oss" else KD) for name, _, _ in uses if name[0] in ("ssq", "oss", "yss")]

    with ExitStack() as stack:
        def sb(name, shape, dt=F32):
            return stack.enter_context(nc.sbuf_tensor(name, shape, dt))

        def sem(name):
            return stack.enter_context(nc.semaphore(name))

        ring = sb("ring", [P, ESLOTS * PIECE])
        xT = sb("xT", [P, KD, TOK])
        hT = sb("hT", [P, KD, TOK])
        mixT = sb("mixT", [P, KD, TOK])
        work = sb("work", [P, 14336])
        sq = sb("sq", [P, 2, TOK])
        rs = sb("rs", [P, 2, TOK])
        tmp = sb("tmp", [P, 2, TOK])
        ident = sb("ident", [P, P])
        ones = sb("ones", [P, P])
        masks = sb("masks", [P, len(LEVELS), P], U8)
        first0 = sb("first0", [P, TOK], U8)
        last0 = sb("last0", [P, TOK], U8)
        vecs = sb("vecs", [P, DEPTH, VROWS])
        modv = sb("modv", [P, DEPTH, 6, KD, 2])
        csil = sb("csil", [P, KD, 2])
        wdec = sb("wdec", [2 * RANK, DEPTH, HEADS * DK])
        rank_rows = sb("rank_rows", [2 * RANK, 2])
        dec = sb("dec", [P, 2, RT, NCH])
        wr = sb("wr", [P, KD, NE])
        small = sb("small", [P, 16, NE])
        cnt_i = sb("cnt_i", [1, NE], I32)
        eps = sb("eps", [P, 1])
        one = sb("one", [P, 1])
        ps = [stack.enter_context(nc.psum_tensor(f"ps{i}", [P, 512], F32)) for i in range(8)]

        def part(at, *dims, dt=None):
            n = int(np.prod(dims))
            a = work[:, at:at + n]
            if len(dims) == 2:
                a = a.rearrange("p (a b) -> p a b", a=dims[0])
            if len(dims) == 3:
                a = a.rearrange("p (a b c) -> p a b c", a=dims[0], b=dims[1])
            if len(dims) == 4:
                a = a.rearrange("p (a b c d) -> p a b c d", a=dims[0], b=dims[1], c=dims[2])
            return a

        qT = part(0, RT, TOK)
        kT = part(1024, RT, TOK)
        vtok = part(2048, NG, HEADS * DV)
        la = part(4096, 2, RT, TOK)
        kdt = part(4096, 2, NG, HEADS * DK)
        cum = part(6144, 2, RT, TOK)
        lvl = part(8192, 2, 2, RT, TOK)
        att = part(12288, 4, 4, P)
        a2 = work[0:2 * RANK, 12288:12288 + 2 * TOK].rearrange("p (a b) -> p a b", a=2)
        states = hT[:, :, :].rearrange("p a b -> p (a b)").rearrange("p (d c r v) -> p d c r v", d=2, c=NCH, r=RT)
        ffh = part(0, JF, TOK)
        htok = part(0, TT, D)
        xsel = part(2048, KD, 256)
        ye = part(4096, KD, 256)
        yslot = part(6144, 2, D)
        swt = part(8192, 2, SEQ)
        selg = part(8704, TT, 256)
        selw = part(9216, TT, 256)
        yacc = part(9728, KD, SEQ)
        esg = part(11776, 2, 256)
        eh = part(12288, 2, 256)
        slotno = part(12800, 256)
        before = part(13056, P)
        tie = part(13184, NE * NE)
        route = part(13568, 2, NE * NE)
        zeros = work[:, 13312:13312 + 256].bitcast(BF16)
        vrow = part(0, DEPTH, P)
        xrow = mixT[:, :, :].rearrange("p a b -> p (a b)").rearrange("p (t d) -> p t d", t=NG)
        iota_i = work[:, 1024:1024 + P].bitcast(I32)
        iota_j = work[:, 1152:1152 + P].bitcast(I32)
        ixor = work[:, 1280:1280 + P].bitcast(I32)
        iota_t = work[:, 1408:1408 + TOK].bitcast(I32)
        iota_r = work[0:2 * RANK, 1920:1921].bitcast(I32)
        itmp = work[:, 2048:2048 + P]
        iota_s = work[:, 11776:11776 + 256].bitcast(I32)
        iota_b = work[:, 12032:12032 + P].bitcast(I32)
        iota_e = work[:, 12160:12160 + NE * NE].bitcast(I32)
        osb = hT[:, :, :].rearrange("p a b -> p (a b)").rearrange("p (t d) -> p t d", t=NG)

        def slot(name):
            i = chunk_at[name] % SLOTS
            return ring[:, i * CHUNKW:(i + 1) * CHUNKW]

        tile_ready = sem("tile_ready")
        drained = [sem(f"bank{i}_drained") for i in range(8)]
        chunk_in = [sem(f"chunk_in{i}") for i in range(SLOTS)]
        rows_in = sem("rows_in")
        consts_in = sem("consts_in")
        vrow_clear = sem("vrow_clear")
        iota_done = sem("iota_done")
        consts_done = sem("consts_done")
        csil_ready = sem("csil_ready")
        sq_ready = sem("sq_ready")
        sq_used = sem("sq_used")
        std_ready = sem("std_ready")
        rs_used = sem("rs_used")
        mod_ready = sem("mod_ready")
        h_ready = sem("h_ready")
        res_ready = sem("res_ready")
        lnz_ready = sem("lnz_ready")
        cum_ready = sem("cum_ready")
        diff_ready = sem("diff_ready")
        decay_ready = sem("decay_ready")
        level_ready = sem("level_ready")
        state_diff = sem("state_diff")
        state_exp = sem("state_exp")
        state_ops = sem("state_ops")
        states_ready = sem("states_ready")
        conv_read = sem("conv_read")
        gate_ready = sem("gate_ready")
        mix_ready = sem("mix_ready")
        sg_ready = sem("sg_ready")
        vstep = sem("vector_step")
        astep = sem("scalar_step")
        ex_ready = sem("expert_exp")
        logits_in = sem("logits_in")
        sel_counted = sem("selection_ready")
        route_ready = sem("route_ready")
        iota2_done = sem("iota2_done")
        consts2_done = sem("consts2_done")
        piece_in = [sem(f"piece_in{i}") for i in range(ESLOTS)]
        piece_free = [sem(f"piece_free{i}") for i in range(ESLOTS)]
        sel_ready = sem("sel_ready")
        misc_ready = sem("misc_ready")
        misc_drained = sem("misc_drained")
        y_drained = sem("y_drained")
        gu_ready = sem("gu_ready")
        gu_drained = sem("gu_drained")
        esg_ready = sem("esg_ready")
        stored = sem("stored")

        sq_free, rs_free = [], []
        passed = [0, 0]
        for name, tiles in sums:
            for k in range(tiles - 1):
                passed[0] += 1
                sq_free.append((sq_used, passed[0]))
            sq_free.append((tile_ready, tile_at[name] + 1))
            if name[0] == "oss":
                o = ("o", *name[1:])
                rs_free.append((drained[bank_of[o]], nth_of[o] + 1))
            else:
                passed[1] += 1
                rs_free.append((rs_used, passed[1]))

        block = stack.enter_context(nc.Block())

        def wait_tile(eng, name):
            eng.wait_ge(tile_ready, tile_at[name] + 1)

        def wait_drained(eng, name):
            eng.wait_ge(drained[bank_of[name]], nth_of[name] + 1)

        def drains(ins, name):
            ins.then_inc(drained[bank_of[name]], 1)

        def bank(name):
            return ps[bank_of[name]]

        def first_col(L):
            return 0 if L == 0 else CTX

        def rows(w, a, n):
            return w[:, a:a + n].rearrange("(k p) n -> p k n", p=P)

        @block.sync
        def _(sp):
            for t in range(NG):
                src = ctx_in[0] if t < 2 else x[0]
                sp.dma_start(xrow[:, t, :], src[(t % 2) * P:(t % 2 + 1) * P, :]).then_inc(rows_in, 16)
            for i, ch in enumerate(chunk_order):
                if i >= SLOTS:
                    sp.wait_ge(tile_ready, chunk_last[chunk_order[i - SLOTS]] + 1)
                kind = ch[0]
                dst = slot(ch)
                full = chunk_in[i % SLOTS]
                d3 = dst.rearrange("p (k n) -> p k n", k=KD)
                if kind == "mod":
                    sp.dma_start(d3, rows(w_mod[ch[1]], 512 * ch[2], 512)).then_inc(full, 16)
                elif kind == "a":
                    sp.dma_start(d3[:, :, 0:2 * RANK], rows(w_in[ch[1]], COL["a"], 2 * RANK)).then_inc(full, 16)
                elif kind in COL:
                    sp.dma_start(d3, rows(w_in[ch[1]], COL[kind], 512)).then_inc(full, 16)
                elif kind == "wo":
                    sp.dma_start(d3, rows(w_out[ch[1]], 512 * ch[2], 512)).then_inc(full, 16)
                elif kind == "ff":
                    d4 = dst.rearrange("p (w k n) -> p w k n", w=2, k=KD)
                    sp.dma_start(d4[:, 0], rows(w1[0], 256 * ch[1], 256)).then_inc(full, 16)
                    sp.dma_start(d4[:, 1], rows(w3[0], 256 * ch[1], 256)).then_inc(full, 16)
                else:
                    k0 = 8 * ch[2]
                    nk = min(8, JF - k0)
                    src = rows(w2[0][k0 * P:(k0 + nk) * P], 512 * ch[1], 512)
                    sp.dma_start(d3[:, 0:nk], src).then_inc(full, 16)
            sp.wait_ge(tile_ready, chunk_last[chunk_order[-1]] + 1)
            for s in range(ESLOTS):
                sp.sem_inc(piece_free[s], 1)
            with sp.Fori(0, NE) as e:
                with sp.Fori(0, JE // ESLOTS) as r:
                    for s in range(ESLOTS):
                        sp.wait_ge(piece_free[s], e * (JE // ESLOTS) + r + 1)
                        dst = ring[:, s * PIECE:(s + 1) * PIECE]
                        cols = bass.ds(r * (ESLOTS * P) + s * P, P)
                        for w, src in ((0, e_w1), (1, e_w3)):
                            sp.dma_start(
                                dst[:, w * D:(w + 1) * D].rearrange("p (k n) -> p k n", k=KD),
                                src[0, bass.ds(e, 1), :, cols].rearrange("a (k p) n -> p (a k) n", p=P),
                            ).then_inc(piece_in[s], 16)
                        sp.dma_start(dst[:, 2 * D:3 * D],
                                     e_w2[0, bass.ds(e, 1), cols, :].rearrange("a p n -> p (a n)"),
                                     ).then_inc(piece_in[s], 16)
            for i in range(4):
                wait_drained(sp, ("out", i))
                sp.dma_start(out[0, (i // 2) * P:(i // 2 + 1) * P, (i % 2) * 512:(i % 2 + 1) * 512],
                             osb[:, i // 2, (i % 2) * 512:(i % 2 + 1) * 512]).then_inc(stored, 16)
            sp.wait_ge(stored, 64)

        @block.gpsimd
        def _(pool):
            pool.memset(vrow, 0.0).then_inc(vrow_clear, 1)
            pool.iota(iota_i, pattern=[[1, P]], base=0, channel_multiplier=0).then_inc(iota_done, 1)
            pool.iota(iota_j, pattern=[[0, P]], base=0, channel_multiplier=1).then_inc(iota_done, 1)
            pool.iota(iota_t, pattern=[[0, NCH], [1, CHUNK]], base=0, channel_multiplier=0).then_inc(iota_done, 1)
            pool.iota(iota_r, pattern=[[1, 1]], base=0, channel_multiplier=1).then_inc(iota_done, 1)
            wait_drained(pool, ("y", DEPTH - 1, 0))
            pool.iota(iota_s, pattern=[[1, 256]], base=0, channel_multiplier=0).then_inc(iota2_done, 1)
            pool.iota(iota_b, pattern=[[1, P]], base=0, channel_multiplier=-1).then_inc(iota2_done, 1)
            pool.iota(iota_e, pattern=[[1, NE], [-1, NE]], base=0, channel_multiplier=0).then_inc(iota2_done, 1)

        @block.tensor
        def _(pe):
            at = [0]

            def begin(name):
                assert tile_at[name] == at[0], name
                if nth_of[name]:
                    pe.wait_ge(drained[bank_of[name]], nth_of[name])
                return bank(name)

            def end(ins):
                ins.then_inc(tile_ready, 1)
                at[0] += 1

            def weights(ch, **dims):
                pe.wait_ge(chunk_in[chunk_at[ch] % SLOTS], chunk_value[ch])
                if not dims:
                    dims = {"k": KD}
                names = " ".join(dims)
                return slot(ch).rearrange(f"p ({names} n) -> p {names} n", **dims)

            nsq = [0]

            def add_square(name, k, tiles, n):
                if k == 0 and nth_of[name]:
                    pe.wait_ge(drained[bank_of[name]], nth_of[name])
                pe.wait_ge(sq_ready, nsq[0] + 1)
                ins = pe.matmul(bank(name)[:, 0:n], ones[:], sq[:, nsq[0] % 2, 0:n],
                                start=(k == 0), stop=(k == tiles - 1))
                if k < tiles - 1:
                    ins.then_inc(sq_used, 1)
                else:
                    assert tile_at[name] == at[0], name
                    end(ins)
                nsq[0] += 1

            def square_sum(name, tiles, n):
                for k in range(tiles):
                    add_square(name, k, tiles, n)

            def mod(layer, s):
                acc = begin(("mod", layer, s))
                for half in range(2):
                    w = weights(("mod", layer, 2 * s + half))
                    for m in range(4):
                        o = 2 * (4 * half + m)
                        for k in range(KD):
                            ins = pe.matmul(acc[:, o:o + 2], w[:, k, m * P:(m + 1) * P], csil[:, k, :],
                                            start=(k == 0), stop=(k == KD - 1))
                end(ins)

            def project(name, w, m, c0, norm, width=P):
                acc = begin(name)
                for k in range(KD):
                    pe.wait_ge(h_ready, norm * KD + k + 1)
                    ins = pe.matmul(acc[0:width, 0:TOK - c0], w[:, k, m * P:m * P + width], hT[:, k, c0:],
                                    start=(k == 0), stop=(k == KD - 1))
                end(ins)

            pe.wait_ge(consts_done, 1)
            pe.wait_ge(consts_in, 16 * 23)
            for L in range(DEPTH):
                acc = begin(("vec", L))
                end(pe.transpose(acc[:, 0:VROWS], vrow[0:VROWS, L, :], ident[0:VROWS, 0:VROWS]))
            pe.wait_ge(rows_in, 16 * NG)
            for k in range(KD):
                acc = begin(("xt", k))
                for t in range(NG):
                    ins = pe.transpose(acc[:, t * P:(t + 1) * P], xrow[:, t, k * P:(k + 1) * P], ident[:])
                end(ins)
            pe.wait_ge(csil_ready, 2)
            for s in range(6):
                mod(0, s)

            for L in range(DEPTH):
                c0 = first_col(L)
                n = TOK - c0
                groups = range(c0 // P, NG)
                square_sum(("ssq", 2 * L), KD, TOK)
                w = weights(("qk", L))
                for m in range(RT):
                    project(("q", L, m), w, m, c0, 2 * L)
                for m in range(RT):
                    project(("k", L, m), w, RT + m, 0, 2 * L)
                project(("a", L), weights(("a", L)), 0, 0, 2 * L, width=2 * RANK)
                wait_drained(pe, ("a", L))
                for i in range(4):
                    acc = begin(("z", L, i))
                    end(pe.matmul(acc[:], wdec[:, L, (i % 2) * P:(i % 2 + 1) * P], a2[:, i // 2, :],
                                  start=True, stop=True))
                w = weights(("v", L))
                for g in range(NG):
                    acc = begin(("v", L, g))
                    for k in range(KD):
                        ins = pe.matmul(acc[:], hT[:, k, g * P:(g + 1) * P], w[:, k, :],
                                        start=(k == 0), stop=(k == KD - 1))
                    end(ins)

                def scores(s, key, query):
                    for b in range(c0 // P, 4):
                        acc = begin(("P", L, s, b))
                        for gi in range(2):
                            for r in range(RT):
                                rows_ = slice(DK * (b % 2), DK * (b % 2) + DK)
                                g = 2 * (b // 2) + gi
                                o = (2 * gi + r) * P
                                ins = pe.matmul(acc[:, o:o + P], key[rows_, r, g * P:(g + 1) * P],
                                                query[rows_, r, g * P:(g + 1) * P], start=True, stop=True)
                        end(ins)

                scores(0, kT, qT)
                for s in range(len(LEVELS)):
                    if s < 2:
                        for m in (2 * s, 2 * s + 1):
                            project(("g", L, m), weights(("g", L)), m, c0, 2 * L)
                    else:
                        for kind in "ChB":
                            project((kind, L, s - 2), weights((kind, L)), s - 2, c0, 2 * L)
                    pe.wait_ge(level_ready, 2 * (len(LEVELS) * L + s + 1))
                    scores(s + 1, lvl[:, s % 2, 1], lvl[:, s % 2, 0])
                if L == 0:
                    mod(1, 0)
                    mod(1, 1)
                pe.wait_ge(state_ops, 4 * L + 2)
                for i in range(4):
                    acc = begin(("kt", L, i))
                    for gi in range(2):
                        for r in range(RT):
                            g = 2 * (i % 2) + gi
                            o = (2 * gi + r) * P
                            ins = pe.transpose(acc[:, o:o + P], lvl[:, 0, i // 2, r, g * P:(g + 1) * P], ident[:])
                    end(ins)
                if L == 0:
                    mod(1, 2)
                for d in range(2):
                    for i in range(4):
                        wait_drained(pe, ("kt", L, 2 * d + (i // 2)))
                        acc = begin(("U", L, d, i))
                        for j in range(2):
                            ch = 4 * (i // 2) + i % 2 + 2 * j
                            g, base = ch // 2, CHUNK * (ch % 2)
                            for r in range(RT):
                                for p in range(2):
                                    h = 2 * r + p
                                    ins = pe.matmul(
                                        acc[DK * p:DK * p + DK, (2 * j + r) * DV:(2 * j + r + 1) * DV],
                                        kdt[base:base + CHUNK, d, g, h * DK:(h + 1) * DK],
                                        vtok[base:base + CHUNK, g, h * DV:(h + 1) * DV], start=True, stop=True)
                        end(ins)
                if L == 0:
                    mod(1, 3)
                    mod(1, 4)
                for b in range(c0 // P, 4):
                    wait_drained(pe, ("P", L, len(LEVELS), b))
                pe.wait_ge(states_ready, L + 1)
                pe.wait_ge(state_ops, 4 * L + 4)
                for h in range(HEADS):
                    acc = begin(("o", L, h))
                    p, r = h % 2, h // 2
                    rows_ = slice(DK * p, DK * p + DK)
                    for g in groups:
                        b = 2 * (g // 2) + p
                        pe.matmul(acc[:, g * P - c0:(g + 1) * P - c0], vtok[:, g, h * DV:(h + 1) * DV],
                                  att[:, b, 2 * (g % 2) + r, :], start=True, stop=False, skip_group_check=True)
                        for d in range(2):
                            for ch in (2 * g, 2 * g + 1):
                                if (d == 0 and ch == 0) or (d == 1 and ch == NCH // 2 - 1):
                                    continue
                                o = ch * CHUNK
                                ins = pe.matmul(acc[:, o - c0:o - c0 + CHUNK], states[rows_, d, ch, r, :],
                                                lvl[rows_, 1, d, r, o:o + CHUNK], start=False, stop=True,
                                                skip_group_check=True)
                    end(ins)
                if L == 0:
                    mod(1, 5)
                for h in range(HEADS):
                    square_sum(("oss", L, h), 1, n)
                for m in range(KD):
                    w = weights(("wo", L, m // 4))
                    acc = begin(("y", L, m))
                    for i, k in enumerate((4, 5, 6, 7, 0, 1, 2, 3)):
                        if k < HEADS:
                            pe.wait_ge(mix_ready, HEADS * L + k + 1)
                        else:
                            wait_drained(pe, ("B", L, k - HEADS))
                        ins = pe.matmul(acc[:, 0:n], w[:, k, (m % 4) * P:(m % 4 + 1) * P], mixT[:, k, c0:],
                                        start=(i == 0), stop=(i == KD - 1))
                    end(ins)
                    if m:
                        add_square(("yss", 2 * L), m - 1, KD, n)
                add_square(("yss", 2 * L), KD - 1, KD, n)
                square_sum(("ssq", 2 * L + 1), KD, n)
                if L == 0:
                    for j in range(JF):
                        w = weights(("ff", j // 2), w=2, k=KD)
                        project(("ffg", j), w[:, 0], j % 2, 0, 1)
                        project(("ffu", j), w[:, 1], j % 2, 0, 1)
                    for half in range(2):
                        accs = []
                        for m in range(4):
                            name = ("y2", 4 * half + m)
                            pe.wait_ge(drained[bank_of[name]], nth_of[name])
                            accs.append(bank(name))
                        for i in range(3):
                            w = weights(("w2", half, i))
                            for k in range(8 * i, min(8 * i + 8, JF)):
                                wait_drained(pe, ("ffu", k))
                                for m in range(4):
                                    ins = pe.matmul(accs[m][:], w[:, k - 8 * i, m * P:(m + 1) * P], ffh[:, k, :],
                                                    start=(k == 0), stop=(k == JF - 1))
                                    if k == JF - 1:
                                        end(ins)
                            if half == 1 and i == 0:
                                for m in range(4):
                                    add_square(("yss", 1), m, KD, TOK)
                    for m in range(4, KD):
                        add_square(("yss", 1), m, KD, TOK)

            acc = begin(("lg",))
            for t in range(TT):
                for k in range(KD):
                    pe.wait_ge(h_ready, 3 * KD + k + 1)
                    ins = pe.matmul(acc[:, t * NE:(t + 1) * NE], hT[:, k, CTX + t * P:CTX + (t + 1) * P], wr[:, k, :],
                                    start=(k == 0), stop=(k == KD - 1))
            end(ins)
            for i in range(4):
                acc = begin(("ht", i))
                for j in range(4):
                    k = 4 * (i % 2) + j
                    o = CTX + (i // 2) * P
                    ins = pe.transpose(acc[:, j * P:(j + 1) * P], hT[:, k, o:o + P], ident[:])
                end(ins)
            pe.wait_ge(sel_counted, 1)
            pe.wait_ge(consts2_done, 3)
            sel = small[:, 0:2, :]
            acc = begin(("pos",))
            pe.matmul(acc[:, 0:NE], before, sel[:, 0, :], start=True, stop=True)
            pe.matmul(acc[:, NE:2 * NE], ones[:], sel[:, 0, :], start=True, stop=False)
            pe.matmul(acc[:, NE:2 * NE], before, sel[:, 1, :], start=False, stop=True)
            pe.matmul(acc[:, 2 * NE:3 * NE], ones[:], sel[:, 0, :], start=True, stop=False)
            end(pe.matmul(acc[:, 2 * NE:3 * NE], ones[:], sel[:, 1, :], start=False, stop=True))
            for b in range(8):
                pe.wait_ge(drained[b], max(nth_of[n] for n in tile_at if bank_of[n] == b and tile_at[n] < at[0]) + 1)
            pe.wait_ge(route_ready, 1)

            def expert(e, W):
                sh_n = (W + P - 1) // P
                wp = min(W, P)

                def misc(i):
                    pe.wait_ge(misc_drained, e * MISC + (i + 1))
                    return ps[6 + i % 2]

                pe.wait_ge(sel_ready, e * 4 + 4)
                for i in range(4):
                    acc = misc(i)
                    for m in (2 * i, 2 * i + 1):
                        o = (m % 2) * 256
                        for t in range(TT):
                            ins = pe.matmul(acc[:, o:o + W], htok[:, t, m * P:(m + 1) * P], selg[:, t, 0:W],
                                            start=(t == 0), stop=(t == TT - 1))
                    ins.then_inc(misc_ready, 1)
                for t in range(TT):
                    acc = misc(4 + t)
                    for s in range(sh_n):
                        ins = pe.transpose(acc[:, s * P:(s + 1) * P], selw[:, t, s * P:(s + 1) * P], ident[:])
                    ins.then_inc(misc_ready, 1)
                pe.wait_ge(misc_drained, e * MISC + (4 + 2))
                pe.wait_ge(y_drained, e * 4 + 1)
                for b in range(4):
                    pe.matmul(ps[b][:], zeros[:, 0:P], zeros, start=True, stop=True, skip_group_check=True)
                with pe.Fori(0, JE // BODY) as q:
                    def hidden(j):
                        s = j % ESLOTS
                        pe.wait_ge(piece_in[s], e * (48 * JE // ESLOTS) + q * (48 * BODY // ESLOTS)
                                   + 48 * (j // ESLOTS + 1))
                        pe.wait_ge(gu_drained, e * JE + q * BODY + (j + 1))
                        acc = ps[4 + j % 2]
                        for w in range(2):
                            piece = ring[:, s * PIECE + w * D:s * PIECE + (w + 1) * D]
                            for k in range(KD):
                                ins = pe.matmul(acc[:, 256 * w:256 * w + W], piece[:, k * P:(k + 1) * P],
                                                xsel[:, k, 0:W], start=(k == 0), stop=(k == KD - 1))
                        ins.then_inc(gu_ready, 1)

                    def down(j):
                        s = j % ESLOTS
                        pe.wait_ge(gu_drained, e * JE + q * BODY + (j + 3))
                        piece = ring[:, s * PIECE + 2 * D:s * PIECE + 3 * D]
                        for m in range(KD):
                            o = (m % 2) * 256
                            ins = pe.matmul(ps[m // 2][:, o:o + W], piece[:, m * P:(m + 1) * P], eh[:, j % 2, 0:W],
                                            start=False, stop=True, skip_group_check=True)
                        ins.then_inc(piece_free[s], 1)

                    hidden(0)
                    for j in range(1, BODY):
                        hidden(j)
                        down(j - 1)
                    down(BODY - 1)

                pe.wait_ge(y_drained, e * 4 + 5)
                for i in range(4):
                    acc = misc(6 + i)
                    for s in range(sh_n):
                        for mi in range(2):
                            ins = pe.transpose(acc[:, s * 256 + mi * P:s * 256 + (mi + 1) * P],
                                               ye[:, 2 * i + mi, s * P:(s + 1) * P], ident[:])
                    ins.then_inc(misc_ready, 1)
                for i in range(4):
                    acc = misc(10 + i)
                    pe.wait_ge(misc_drained, e * MISC + (6 + i + 3))
                    for mi in range(2):
                        m = 2 * i + mi
                        for s in range(sh_n):
                            ins = pe.matmul(acc[:, mi * 256:(mi + 1) * 256], yslot[0:wp, s, m * P:(m + 1) * P],
                                            swt[0:wp, s, :], start=(s == 0), stop=(s == sh_n - 1))
                    ins.then_inc(misc_ready, 1)

            with pe.Fori(0, NE) as e:
                chosen = pe.value_load(cnt_i[0:1, bass.ds(e, 1)], min_val=0, max_val=SEQ)
                by_width(pe, chosen, lambda W: expert(e, W))

            pe.wait_ge(misc_drained, NE * MISC + 2)
            square_sum(("yss", 3), KD, SEQ)
            for i in range(4):
                acc = begin(("out", i))
                for j in range(4):
                    k = 4 * (i % 2) + j
                    pe.wait_ge(res_ready, 3 * KD + k + 1)
                    o = CTX + (i // 2) * P
                    ins = pe.transpose(acc[:, j * P:(j + 1) * P], xT[:, k, o:o + P], ident[:])
                end(ins)

        @block.scalar
        def _(act):
            act.wait_ge(vrow_clear, 1)
            for L in range(DEPTH):
                for at_, n, src in ((BM, 48, b_mod[L]), (GMP, 8, g_mix_pre[L]), (GMO, 8, g_mix_post[L]),
                                    (GFP, 8, g_ffn_pre[L]), (GFO, 8, g_ffn_post[L]), (GN, 1, gla_norm[L])):
                    act.dma_start(vrow[at_:at_ + n, L, :], src.rearrange("(r p) -> r p", p=P)).then_inc(consts_in, 16)
                act.dma_start(vrow[BD:BD + 4, L, :],
                              b_decay[L].rearrange("d (r p) -> (d r) p", p=P)).then_inc(consts_in, 16)
                act.dma_start(vrow[CW:CW + 12, L, :],
                              conv_w[L].rearrange("d (r p) -> (d r) p", p=P)).then_inc(consts_in, 16)
                act.dma_start(wdec[:, L, :], w_decay[L].rearrange("d r n -> (d r) n")).then_inc(consts_in, 16)
                if L == 0:
                    act.dma_start(vrow[CC:CC + 8, 0, :], c_ctx.rearrange("(r p) -> r p", p=P)).then_inc(consts_in, 16)
                    act.dma_start(vrow[CX:CX + 8, 0, :],
                                  c.rearrange("a (r p) -> (a r) p", p=P)).then_inc(consts_in, 16)
                    act.dma_start(vrow[CC:CC + 8, 1, :], c_ctx.rearrange("(r p) -> r p", p=P)).then_inc(consts_in, 16)
                    act.dma_start(vrow[CX:CX + 8, 1, :],
                                  c.rearrange("a (r p) -> (a r) p", p=P)).then_inc(consts_in, 16)
            act.dma_start(wr[:], w_router[0].rearrange("(k p) e -> p k e", p=P)).then_inc(consts_in, 16)

            n_sq = [0]
            n_rs = [0]
            steps = [0]

            def step(ins):
                steps[0] += 1
                ins.then_inc(astep, 1)
                return steps[0]

            def square(src, n):
                i = n_sq[0]
                if i >= 2:
                    act.wait_ge(*sq_free[i - 2])
                act.activation(sq[:, i % 2, 0:n], src, ACT.Square).then_inc(sq_ready, 1)
                n_sq[0] += 1

            def std(name, n, width):
                wait_tile(act, name)
                i = n_rs[0]
                if i >= 2:
                    act.wait_ge(*rs_free[i - 2])
                drains(act.activation(rs[:, i % 2, 0:n], bank(name)[:, 0:n], ACT.Sqrt, scale=1.0 / width, bias=eps[:]),
                       name)
                n_rs[0] += 1

            for L in range(DEPTH):
                wait_tile(act, ("vec", L))
                drains(act.copy(vecs[:, L, :], bank(("vec", L))[:, 0:VROWS]), ("vec", L))
            wait_drained(act, ("vec", 0))
            act.activation(csil[:, :, 0], vecs[:, 0, CC:CC + 8], ACT.Silu).then_inc(csil_ready, 1)
            act.activation(csil[:, :, 1], vecs[:, 0, CX:CX + 8], ACT.Silu).then_inc(csil_ready, 1)
            for k in range(KD):
                wait_tile(act, ("xt", k))
                drains(act.copy(xT[:, k, :], bank(("xt", k))[:]), ("xt", k))
            act.wait_ge(consts_done, 1)

            for L in range(DEPTH):
                c0 = first_col(L)
                n = TOK - c0
                v = vecs[:, L, :]
                for k in range(KD):
                    if L == 0:
                        wait_drained(act, ("xt", k))
                    else:
                        act.wait_ge(res_ready, (2 * L - 1) * KD + k + 1)
                    square(xT[:, k, :], TOK)
                std(("ssq", 2 * L), TOK, D)
                for m in range(RT):
                    wait_tile(act, ("q", L, m))
                    drains(act.mul(qT[:, m, c0:], bank(("q", L, m))[:, 0:n], DK ** -0.5), ("q", L, m))
                for m in range(RT):
                    wait_tile(act, ("k", L, m))
                    drains(act.copy(kT[:, m, :], bank(("k", L, m))[:]), ("k", L, m))
                for i in range(4):
                    wait_tile(act, ("z", L, i))
                    drains(act.activation(la[:, i // 2, i % 2, :], bank(("z", L, i))[:], ACT.Identity,
                                          bias=v[:, BD + i:BD + i + 1]), ("z", L, i))
                e4 = lvl[:, 0].rearrange("p a r t -> p (a r) t")
                for i in range(4):
                    wait_drained(act, ("z", L, i))
                    step(act.activation(e4[:, i, :], la[:, i // 2, i % 2, :], ACT.Abs))
                act.wait_ge(astep, steps[0])
                step(act.activation(lvl[:, 0], lvl[:, 0], ACT.Exp, scale=-1.0))
                act.wait_ge(astep, steps[0])
                act.activation(lvl[:, 0], lvl[:, 0], ACT.Ln, bias=one[:]).then_inc(lnz_ready, 1)
                for g in range(NG):
                    wait_tile(act, ("v", L, g))
                    drains(act.copy(vtok[:, g, :], bank(("v", L, g))[:]), ("v", L, g))
                for s in range(len(LEVELS)):
                    for side in range(2):
                        act.wait_ge(diff_ready, 4 * (len(LEVELS) * L + s) + 2 * side + 2)
                        buf = lvl[:, s % 2, side, :, c0:]
                        act.activation(buf, buf, ACT.Exp, scale=1.0 / GATE_NORM).then_inc(decay_ready, 1)
                    if s < 2:
                        for m in (2 * s, 2 * s + 1):
                            wait_tile(act, ("g", L, m))
                            drains(act.copy(mixT[:, m, c0:], bank(("g", L, m))[:, 0:n]), ("g", L, m))
                    else:
                        wait_tile(act, ("C", L, s - 2))
                        if s > 2:
                            act.wait_ge(conv_read, 4 * L + s - 2)
                        drains(act.copy(tmp[:, 0, 0:n], bank(("C", L, s - 2))[:, 0:n]), ("C", L, s - 2))
                for d in range(2):
                    act.wait_ge(state_diff, 2 * L + d + 1)
                    act.activation(lvl[:, 0, d], lvl[:, 0, d], ACT.Exp, scale=1.0 / GATE_NORM).then_inc(state_exp, 1)
                wait_tile(act, ("P", L, len(LEVELS), 3))
                for d in range(2):
                    act.activation(lvl[:, 1, d, :, c0:], cum[:, d, :, c0:], ACT.Exp,
                                   scale=1.0 / GATE_NORM).then_inc(state_exp, 1)
                for d in range(2):
                    edge = CHUNK - 1 if d == 0 else 0
                    ends = cum[:, d].rearrange("p r (c t) -> p r c t", t=CHUNK)[:, :, :, edge]
                    act.activation(dec[:, d], ends, ACT.Exp, scale=1.0 / GATE_NORM).then_inc(state_exp, 1)
                for i in range(4):
                    wait_tile(act, ("kt", L, i))
                    g0 = 2 * (i % 2)
                    drains(act.copy(kdt[:, i // 2, g0:g0 + 2, :],
                                    bank(("kt", L, i))[:].rearrange("p (g n) -> p g n", g=2)), ("kt", L, i))
                for m in range(HEADS):
                    wait_drained(act, ("g", L, m))
                    act.activation(mixT[:, m, c0:], mixT[:, m, c0:], ACT.Silu).then_inc(gate_ready, 1)
                for h in range(HEADS):
                    wait_tile(act, ("o", L, h))
                    square(bank(("o", L, h))[:, 0:n], n)
                for h in range(HEADS):
                    std(("oss", L, h), n, DV)

                def collect(names, n, c0):
                    for m in range(KD):
                        wait_tile(act, names(m))
                        drains(act.copy(hT[:, m, c0:], bank(names(m))[:, 0:n]), names(m))
                        wait_drained(act, names(m))
                        square(hT[:, m, c0:], n)

                collect(lambda m: ("y", L, m), n, c0)
                std(("yss", 2 * L), n, D)
                for k in range(KD):
                    act.wait_ge(res_ready, 2 * L * KD + k + 1)
                    square(xT[:, k, c0:], n)
                std(("ssq", 2 * L + 1), n, D)
                if L == 0:
                    for j in range(JF):
                        wait_tile(act, ("ffg", j))
                        if j >= 2:
                            wait_drained(act, ("ffu", j - 2))
                        drains(act.activation(tmp[:, j % 2, :], bank(("ffg", j))[:], ACT.Silu), ("ffg", j))
                    collect(lambda m: ("y2", m), n, 0)
                    std(("yss", 1), n, D)

            for i in range(4):
                wait_tile(act, ("ht", i))
                drains(act.copy(htok[:, i // 2, (i % 2) * 512:(i % 2 + 1) * 512], bank(("ht", i))[:]), ("ht", i))
            act.wait_ge(logits_in, 2)
            act.activation(small[:, 4:6, :], small[:, 2:4, :], ACT.Exp).then_inc(ex_ready, 1)
            act.sem_inc(y_drained, 1)
            act.wait_ge(route_ready, 1)

            def expert(e, W):
                with act.Fori(0, JE // BODY) as q:
                    for j in range(BODY):
                        act.wait_ge(gu_ready, e * JE + q * BODY + (j + 1))
                        act.wait_ge(gu_drained, e * JE + q * BODY + (j + 1))
                        act.activation(esg[:, j % 2, 0:W], ps[4 + j % 2][:, 0:W], ACT.Silu).then_inc(esg_ready, 1)
                act.wait_ge(piece_free[ESLOTS - 1], e * (JE // ESLOTS) + (JE // ESLOTS + 1))
                for b in range(4):
                    act.copy(ye[:, 2 * b:2 * b + 2, 0:W],
                             ps[b][:].rearrange("p (m t) -> p m t", m=2)[:, :, 0:W]).then_inc(y_drained, 1)

            with act.Fori(0, NE) as e:
                chosen = act.value_load(cnt_i[0:1, bass.ds(e, 1)], min_val=0, max_val=SEQ)
                by_width(act, chosen, lambda W: expert(e, W))
            act.wait_ge(misc_drained, NE * MISC + 2)
            for k in range(KD):
                square(yacc[:, k, :], SEQ)
            std(("yss", 3), SEQ, D)

        @block.vector
        def _(dve):
            steps = [0]
            n_rs = [0]

            def step(ins):
                steps[0] += 1
                ins.then_inc(vstep, 1)
                return steps[0]

            def wait_step(n=None):
                dve.wait_ge(vstep, steps[0] if n is None else n)

            step(dve.memset(eps[:], EPS))
            step(dve.memset(one[:], 1.0))
            step(dve.memset(ones[:], 1.0))
            dve.wait_ge(iota_done, 4)
            step(dve.tensor_tensor(ixor, iota_i, iota_j, ALU.bitwise_xor))
            step(dve.tensor_scalar(first0[:], iota_t, 0.5, None, ALU.is_gt))
            step(dve.tensor_scalar(last0[:], iota_t, CHUNK - 1.5, None, ALU.is_lt))
            step(dve.tensor_scalar(rank_rows[:, 0:1], iota_r, RANK - 0.5, None, ALU.is_lt))
            step(dve.tensor_scalar(rank_rows[:, 1:2], iota_r, RANK - 0.5, None, ALU.is_gt))
            wait_step()
            step(dve.tensor_scalar(ident[:], ixor, 0.0, None, ALU.is_equal))
            for s, half in enumerate(LEVELS):
                step(dve.tensor_scalar(itmp, ixor, float(2 * half), None, ALU.is_ge))
                wait_step()
                step(dve.scalar_tensor_tensor(out=masks[:, s, :], in0=ixor, scalar=float(half), in1=itmp,
                                              op0=ALU.is_ge, op1=ALU.subtract))
                wait_step()
            dve.tensor_copy(itmp, ident[:]).then_inc(consts_done, 1)

            def normalise(norm, L, src, dst, c0, scale, shift):
                n = TOK - c0
                r = rs[:, n_rs[0] % 2, 0:n]
                wait_drained(dve, sums[n_rs[0]][0])
                step(dve.reciprocal(r, r))
                wait_step()
                for k in range(KD):
                    if k == KD - 1:
                        dve.tensor_tensor(tmp[:, k % 2, 0:n], src[:, k, c0:], r, ALU.mult).then_inc(rs_used, 1)
                        dve.wait_ge(*rs_free[n_rs[0]])
                    else:
                        step(dve.tensor_tensor(tmp[:, k % 2, 0:n], src[:, k, c0:], r, ALU.mult))
                        wait_step()
                    if c0 == 0:
                        step(dve.tensor_scalar(dst[:, k, 0:CTX], tmp[:, k % 2, 0:CTX], scale[:, k, 0:1],
                                               shift[:, k, 0:1], ALU.mult, ALU.add))
                        wait_step()
                    dve.tensor_scalar(dst[:, k, CTX:], tmp[:, k % 2, CTX - c0:n], scale[:, k, 1:2],
                                      shift[:, k, 1:2], ALU.mult, ALU.add).then_inc(h_ready, 1)
                    dve.wait_ge(h_ready, KD * norm + k + 1)
                n_rs[0] += 1

            def add_branch(post, src, c0, gate, off=0):
                n = TOK - c0
                r = rs[:, n_rs[0] % 2, 0:n]
                wait_drained(dve, sums[n_rs[0]][0])
                step(dve.reciprocal(r, r))
                wait_step()
                for k in range(KD):
                    if k == KD - 1:
                        dve.tensor_tensor(tmp[:, k % 2, 0:n], src[:, k, c0 - off:], r, ALU.mult).then_inc(rs_used, 1)
                        dve.wait_ge(*rs_free[n_rs[0]])
                    else:
                        step(dve.tensor_tensor(tmp[:, k % 2, 0:n], src[:, k, c0 - off:], r, ALU.mult))
                        wait_step()
                    if c0 == 0:
                        step(dve.scalar_tensor_tensor(out=xT[:, k, 0:CTX], in0=tmp[:, k % 2, 0:CTX],
                                                      scalar=gate[:, k, 0:1], in1=xT[:, k, 0:CTX],
                                                      op0=ALU.mult, op1=ALU.add))
                        wait_step()
                    dve.scalar_tensor_tensor(out=xT[:, k, CTX:], in0=tmp[:, k % 2, CTX - c0:n],
                                             scalar=gate[:, k, 1:2], in1=xT[:, k, CTX:],
                                             op0=ALU.mult, op1=ALU.add).then_inc(res_ready, 1)
                    dve.wait_ge(res_ready, KD * post + k + 1)
                n_rs[0] += 1

            def take_mod(L, s):
                name = ("mod", L, s)
                wait_drained(dve, ("vec", L))
                wait_tile(dve, name)
                acc = bank(name)[:, 0:2 * KD].rearrange("p (k j) -> p k j", j=2)
                bias = vecs[:, L, BM + 8 * s:BM + 8 * s + 8].unsqueeze(2).broadcast_to([P, KD, 2])
                drains(dve.tensor_tensor(modv[:, L, s], acc, bias, ALU.add), name)
                gain = {1: GMP, 2: GMO, 4: GFP, 5: GFO}.get(s)
                wait_drained(dve, name)
                if gain is not None:
                    g = vecs[:, L, gain:gain + 8].unsqueeze(2).broadcast_to([P, KD, 2])
                    add = 1.0 if s in (1, 4) else 0.0
                    step(dve.scalar_tensor_tensor(out=modv[:, L, s], in0=modv[:, L, s], scalar=add, in1=g,
                                                  op0=ALU.add, op1=ALU.mult))
                    wait_step()

            for s in range(6):
                take_mod(0, s)

            for L in range(DEPTH):
                c0 = first_col(L)
                n = TOK - c0
                v = vecs[:, L, :]
                if L == 0:
                    for k in range(KD):
                        wait_drained(dve, ("xt", k))
                normalise(2 * L, L, xT, hT, 0, modv[:, L, 1], modv[:, L, 0])
                wait_tile(dve, ("a", L))
                acc = bank(("a", L))
                step(dve.tensor_scalar(a2[:, 0, :], acc[0:2 * RANK, :], rank_rows[:, 0:1], None, ALU.mult))
                drains(dve.tensor_scalar(a2[:, 1, :], acc[0:2 * RANK, :], rank_rows[:, 1:2], None, ALU.mult), ("a", L))
                wait_step()
                dve.wait_ge(lnz_ready, L + 1)
                step(dve.scalar_tensor_tensor(out=la.rearrange("p d r t -> p (d r t)"),
                                              in0=la.rearrange("p d r t -> p (d r t)"), scalar=0.0,
                                              in1=lvl[:, 0].rearrange("p a r t -> p (a r t)"),
                                              op0=ALU.min, op1=ALU.subtract))
                wait_step()
                for r in range(RT):
                    step(dve.tensor_tensor_scan(cum[:, 0, r, :], first0[:], la[:, 0, r, :], 0.0, ALU.mult, ALU.add))
                    step(dve.tensor_tensor_scan(cum[:, 1, r, ::-1], last0[:, ::-1], la[:, 1, r, ::-1], 0.0,
                                                ALU.mult, ALU.add))
                wait_step()

                def halves(a, half):
                    return a.rearrange("p r (n two h) -> p r n two h", two=2, h=half)

                def differences(s):
                    half = LEVELS[s]
                    f, b = halves(cum[:, 0, :, c0:], half), halves(cum[:, 1, :, c0:], half)
                    shape = [P, RT, n // (2 * half), half]
                    left_end = f[:, :, :, 0, half - 1:half].broadcast_to(shape)
                    right_end = b[:, :, :, 1, 0:1].broadcast_to(shape)
                    q_, k_ = halves(lvl[:, s % 2, 0, :, c0:], half), halves(lvl[:, s % 2, 1, :, c0:], half)
                    if s >= 2:
                        wait_tile(dve, ("P", L, s - 1, 3))
                    for o, i0, i1 in ((q_[:, :, :, 1], f[:, :, :, 1], left_end),
                                      (q_[:, :, :, 0], b[:, :, :, 0], right_end),
                                      (k_[:, :, :, 0], left_end, f[:, :, :, 0]),
                                      (k_[:, :, :, 1], right_end, b[:, :, :, 1])):
                        dve.tensor_tensor(o, i0, i1, ALU.subtract).then_inc(diff_ready, 1)

                def take_scores(s):
                    for b in range(c0 // P, 4):
                        name = ("P", L, s, b)
                        wait_tile(dve, name)
                        acc = bank(name)[:].rearrange("p (a b) -> p a b", a=4)
                        if s == 0:
                            same = ident[:].unsqueeze(1).broadcast_to([P, 4, P])
                            drains(dve.scalar_tensor_tensor(out=att[:, b], in0=acc, scalar=2.0, in1=same,
                                                            op0=ALU.mult, op1=ALU.mult), name)
                        else:
                            wait_drained(dve, ("P", L, s - 1, b))
                            mask = masks[:, s - 1, :].unsqueeze(1).broadcast_to([P, 4, P])
                            drains(dve.copy_predicated(att[:, b], mask, acc), name)

                def conv(i):
                    dve_h, dve_b = ("h", L, i), ("B", L, i)
                    wait_drained(dve, ("C", L, i))
                    wait_tile(dve, dve_h)
                    u = tmp[:, 1, 0:n]
                    drains(dve.tensor_tensor(u, tmp[:, 0, 0:n], bank(dve_h)[:, 0:n], ALU.mult), dve_h)
                    wait_drained(dve, dve_h)
                    y = mixT[:, HEADS + i, c0:]
                    dve.tensor_scalar(y, u, v[:, CW + 4 + i:CW + 5 + i], None, ALU.mult).then_inc(conv_read, 1)
                    dve.wait_ge(conv_read, 4 * L + i + 1)
                    for tap, dst0, src0 in ((0, 1, 0), (2, 0, 1)):
                        if L == 0:
                            ins = dve.scalar_tensor_tensor(
                                out=y[:, dst0:dst0 + CTX - 1], in0=u[:, src0:src0 + CTX - 1],
                                scalar=v[:, CW + 4 * tap + i:CW + 4 * tap + i + 1],
                                in1=y[:, dst0:dst0 + CTX - 1], op0=ALU.mult, op1=ALU.add)
                            step(ins)
                        us = u[:, CTX - c0:].rearrange("p (s t) -> p s t", t=64)
                        ys = y[:, CTX - c0:].rearrange("p (s t) -> p s t", t=64)
                        step(dve.scalar_tensor_tensor(
                            out=ys[:, :, dst0:dst0 + 63], in0=us[:, :, src0:src0 + 63],
                            scalar=v[:, CW + 4 * tap + i:CW + 4 * tap + i + 1],
                            in1=ys[:, :, dst0:dst0 + 63], op0=ALU.mult, op1=ALU.add))
                        wait_step()
                    wait_tile(dve, dve_b)
                    drains(dve.tensor_tensor(y, y, bank(dve_b)[:, 0:n], ALU.mult), dve_b)

                for m in range(RT):
                    wait_drained(dve, ("q", L, m))
                    wait_drained(dve, ("k", L, m))
                differences(0)
                take_scores(0)
                for s in range(len(LEVELS)):
                    if s + 1 < len(LEVELS):
                        differences(s + 1)
                    for side, t in ((0, qT), (1, kT)):
                        dve.wait_ge(decay_ready, 2 * (len(LEVELS) * L + s) + side + 1)
                        buf = lvl[:, s % 2, side, :, c0:]
                        dve.tensor_tensor(buf, buf, t[:, :, c0:], ALU.mult).then_inc(level_ready, 1)
                    if s > 0:
                        take_scores(s)
                    if s > 2:
                        conv(s - 3)
                wait_tile(dve, ("P", L, len(LEVELS) - 1, 3))
                for d, edge in ((0, CHUNK - 1), (1, 0)):
                    b = cum[:, d].rearrange("p r (c t) -> p r c t", t=CHUNK)
                    dve.tensor_tensor(lvl[:, 0, d].rearrange("p r (c t) -> p r c t", t=CHUNK),
                                      b[:, :, :, edge:edge + 1].broadcast_to([P, RT, NCH, CHUNK]), b,
                                      ALU.subtract).then_inc(state_diff, 1)
                for d in range(2):
                    dve.wait_ge(state_exp, 6 * L + d + 1)
                    dve.tensor_tensor(lvl[:, 0, d], lvl[:, 0, d], kT, ALU.mult).then_inc(state_ops, 1)
                conv(3)
                take_scores(len(LEVELS))
                for d in range(2):
                    dve.wait_ge(state_exp, 6 * L + d + 3)
                    dve.tensor_tensor(lvl[:, 1, d, :, c0:], lvl[:, 1, d, :, c0:], qT[:, :, c0:],
                                      ALU.mult).then_inc(state_ops, 1)
                if L == 0:
                    for s in range(3):
                        take_mod(1, s)
                dve.wait_ge(state_exp, 6 * L + 6)
                for d in range(2):
                    order = list(range(NCH)) if d == 0 else list(range(3, -1, -1)) + list(range(NCH - 1, 3, -1))
                    seen = set()
                    for at_, ch in enumerate(order):
                        i = 2 * (ch // 4) + ch % 2
                        j = (ch % 4) // 2
                        name = ("U", L, d, i)
                        wait_tile(dve, name)
                        acc = bank(name)
                        nxt = order[at_ + 1] if at_ + 1 < NCH else None
                        closes = name in seen
                        seen.add(name)
                        for r in range(RT):
                            add = acc[:, (2 * j + r) * DV:(2 * j + r + 1) * DV]
                            if nxt is None:
                                if r == RT - 1:
                                    ins = dve.tensor_copy(small[:, 14, 0:1], acc[:, 0:1])
                                else:
                                    continue
                            elif at_ == 0:
                                ins = dve.tensor_copy(states[:, d, nxt, r, :], add)
                            else:
                                ins = dve.scalar_tensor_tensor(out=states[:, d, nxt, r, :], in0=states[:, d, ch, r, :],
                                                               scalar=dec[:, d, r, ch:ch + 1], in1=add,
                                                               op0=ALU.mult, op1=ALU.add)
                            if closes and r == RT - 1:
                                drains(ins, name)
                                wait_drained(dve, name)
                            else:
                                step(ins)
                        wait_step()
                dve.tensor_copy(small[:, 14, 1:2], ones[:, 0:1]).then_inc(states_ready, 1)
                if L == 0:
                    for s in range(3, 5):
                        take_mod(1, s)
                if L == 0:
                    take_mod(1, 5)
                for h in range(HEADS):
                    r = rs[:, n_rs[0] % 2, 0:n]
                    wait_drained(dve, sums[n_rs[0]][0])
                    step(dve.reciprocal(r, r))
                    wait_step()
                    t = tmp[:, h % 2, 0:n]
                    name = ("o", L, h)
                    wait_tile(dve, name)
                    drains(dve.tensor_tensor(t, r, bank(name)[:, 0:n], ALU.mult), name)
                    wait_drained(dve, name)
                    dve.wait_ge(gate_ready, HEADS * L + h + 1)
                    dve.scalar_tensor_tensor(out=mixT[:, h, c0:], in0=t, scalar=v[:, GN:GN + 1], in1=mixT[:, h, c0:],
                                             op0=ALU.mult, op1=ALU.mult).then_inc(mix_ready, 1)
                    n_rs[0] += 1
                add_branch(2 * L, hT, c0, modv[:, L, 2])
                normalise(2 * L + 1, L, xT, hT, c0, modv[:, L, 4], modv[:, L, 3])
                if L == 0:
                    for j in range(JF):
                        wait_tile(dve, ("ffu", j))
                        wait_drained(dve, ("ffg", j))
                        drains(dve.tensor_tensor(ffh[:, j, :], tmp[:, j % 2, :], bank(("ffu", j))[:], ALU.mult),
                               ("ffu", j))
                    add_branch(1, hT, 0, modv[:, 0, 5])

            dve.wait_ge(iota2_done, 3)
            dve.tensor_copy(slotno, iota_s).then_inc(consts2_done, 1)
            dve.tensor_scalar(before, iota_b, 0.5, None, ALU.is_gt).then_inc(consts2_done, 1)
            dve.tensor_scalar(tie, iota_e, 0.5, None, ALU.is_gt).then_inc(consts2_done, 1)
            step(dve.memset(zeros, 0.0))
            dve.wait_ge(consts2_done, 3)
            wait_tile(dve, ("lg",))
            lg = small[:, 12:14, :]
            drains(dve.tensor_copy(lg, bank(("lg",))[:, 0:TT * NE].rearrange("p (t e) -> p t e", t=TT)), ("lg",))
            wait_drained(dve, ("lg",))
            top = small[:, 11, 0:TT]
            step(dve.tensor_reduce(top, lg, AX_X, ALU.max))
            wait_step()
            dve.tensor_scalar(small[:, 2, :], lg[:, 0, :], top[:, 0:1], None, ALU.subtract).then_inc(logits_in, 1)
            dve.tensor_scalar(small[:, 3, :], lg[:, 1, :], top[:, 1:2], None, ALU.subtract).then_inc(logits_in, 1)
            sel = small[:, 0:2, :]
            tie3 = tie.rearrange("p (e j) -> p e j", e=NE)
            for t in range(TT):
                mine = lg[:, t, :].unsqueeze(2).broadcast_to([P, NE, NE])
                other = lg[:, t, :].unsqueeze(1).broadcast_to([P, NE, NE])
                larger = route[:, 0, 0:NE * NE].rearrange("p (e j) -> p e j", e=NE)
                equal = route[:, 1, 0:NE * NE].rearrange("p (e j) -> p e j", e=NE)
                step(dve.tensor_tensor(larger, other, mine, ALU.is_gt))
                step(dve.tensor_tensor(equal, other, mine, ALU.is_equal))
                wait_step()
                step(dve.tensor_tensor(equal, equal, tie3, ALU.mult))
                wait_step()
                step(dve.tensor_tensor(larger, larger, equal, ALU.add))
                wait_step()
                step(dve.tensor_reduce(small[:, 10, :], larger, AX_X, ALU.add))
                wait_step()
                ins = dve.tensor_scalar(sel[:, t, :], small[:, 10, :], 1.5, None, ALU.is_lt)
                if t == TT - 1:
                    ins.then_inc(sel_counted, 1)
                    dve.wait_ge(sel_counted, 1)
                else:
                    step(ins)
                    wait_step()
            share = small[:, 6:8, :]
            dve.wait_ge(ex_ready, 1)
            step(dve.tensor_tensor(share, small[:, 4:6, :], sel, ALU.mult))
            wait_step()
            total = small[:, 11, 2:2 + TT]
            step(dve.tensor_reduce(total, share, AX_X, ALU.add))
            wait_step()
            step(dve.reciprocal(total, total))
            wait_step()
            for t in range(TT):
                step(dve.tensor_scalar(share[:, t, :], share[:, t, :], total[:, t:t + 1], None, ALU.mult))
            place = small[:, 8:10, :]
            wait_tile(dve, ("pos",))
            acc = bank(("pos",))
            step(dve.scalar_tensor_tensor(out=place, in0=acc[:, 0:TT * NE].rearrange("p (t e) -> p t e", t=TT),
                                          scalar=1.0, in1=sel, op0=ALU.add, op1=ALU.mult))
            drains(dve.tensor_copy(cnt_i[:], acc[0:1, 2 * NE:3 * NE]), ("pos",))
            wait_step()
            step(dve.tensor_scalar(place, place, 1.0, None, ALU.subtract))
            step(dve.memset(yacc, 0.0))
            step(dve.memset(ye, 0.0))
            wait_step()
            wait_drained(dve, ("pos",))
            dve.tensor_copy(small[:, 14, 2:3], ones[:, 0:1]).then_inc(route_ready, 1)
            dve.sem_inc(misc_drained, 2)
            dve.sem_inc(gu_drained, 2)

            def expert(e, W):
                sh_n = (W + P - 1) // P
                wp = min(W, P)

                def misc(i):
                    dve.wait_ge(misc_ready, e * MISC + (i + 1))
                    return ps[6 + i % 2]

                for i in range(4):
                    acc = misc(i)
                    dve.tensor_copy(xsel[:, 2 * i:2 * i + 2, 0:W],
                                    acc[:].rearrange("p (m t) -> p m t", m=2)[:, :, 0:W]).then_inc(misc_drained, 1)
                for t in range(TT):
                    acc = misc(4 + t)
                    dve.tensor_copy(swt[0:wp, 0:sh_n, t * P:(t + 1) * P],
                                    acc[0:wp, 0:sh_n * P].rearrange("p (s t) -> p s t", s=sh_n),
                                    ).then_inc(misc_drained, 1)
                with dve.Fori(0, JE // BODY) as q:
                    for j in range(BODY):
                        dve.wait_ge(esg_ready, e * JE + q * BODY + (j + 1))
                        dve.tensor_tensor(eh[:, j % 2, 0:W], esg[:, j % 2, 0:W], ps[4 + j % 2][:, 256:256 + W],
                                          ALU.mult).then_inc(gu_drained, 1)
                for i in range(4):
                    acc = misc(6 + i)
                    dve.tensor_copy(yslot[0:wp, 0:sh_n, 2 * i * P:(2 * i + 2) * P],
                                    acc[0:wp, 0:sh_n * 256].rearrange("p (s t) -> p s t", s=sh_n),
                                    ).then_inc(misc_drained, 1)
                for i in range(4):
                    acc = misc(10 + i)
                    dve.wait_ge(misc_drained, e * MISC + (10 + i + 2))
                    dve.tensor_tensor(yacc[:, 2 * i:2 * i + 2, :], yacc[:, 2 * i:2 * i + 2, :],
                                      acc[:].rearrange("p (m t) -> p m t", m=2), ALU.add).then_inc(misc_drained, 1)

            with dve.Fori(0, NE) as e:
                for t in range(TT):
                    one_hot = place[:, t, bass.ds(e, 1)]
                    dve.tensor_scalar(selg[:, t, :], slotno, one_hot, None, ALU.is_equal).then_inc(sel_ready, 1)
                    dve.tensor_scalar(selw[:, t, :], slotno, one_hot, share[:, t, bass.ds(e, 1)],
                                      ALU.is_equal, ALU.mult).then_inc(sel_ready, 1)
                chosen = dve.value_load(cnt_i[0:1, bass.ds(e, 1)], min_val=0, max_val=SEQ)
                by_width(dve, chosen, lambda W: expert(e, W))
            add_branch(3, yacc, CTX, modv[:, 1, 5], off=CTX)
            for i in range(4):
                wait_tile(dve, ("out", i))
                drains(dve.tensor_copy(osb[:, i // 2, (i % 2) * 512:(i % 2 + 1) * 512], bank(("out", i))[:]),
                       ("out", i))


_INS = ["x", "c", "ctx", "c_ctx", "w_mod", "b_mod", "g_mix_pre", "g_mix_post", "w_in", "w_decay", "b_decay",
        "gla_norm", "conv_w", "w_out", "g_ffn_pre", "g_ffn_post", "w1", "w3", "w2", "w_router",
        "e_w1", "e_w3", "e_w2"]


def kernel(**inputs):
    import concourse.bacc as bacc
    from concourse.bass_utils import run_bass_kernel_spmd

    nc = bacc.Bacc("TRN2", target_bir_lowering=False, num_devices=1)
    arrays, args = {}, []
    for name in _INS:
        a = np.ascontiguousarray(inputs[name])
        arrays[f"in_{name}"] = a
        args.append(nc.dram_tensor(f"in_{name}", a.shape, mybir.dt.from_np(a.dtype), kind="ExternalInput").ap())
    args.append(nc.dram_tensor("out_0", (1, SEQ, D), F32, kind="ExternalOutput").ap())
    hybrid_backbone(nc, *args)
    r = run_bass_kernel_spmd(nc, [arrays], core_ids=[0])
    return r.results[0]["out_0"]
```

```python
from contextlib import ExitStack

import numpy as np

import concourse.bass as bass
from concourse import mybir

F32 = mybir.dt.float32
BF16 = mybir.dt.bfloat16
F32R = mybir.dt.float32r
I32 = mybir.dt.int32
U8 = mybir.dt.uint8
ALU = mybir.AluOpType
ACT = mybir.ActivationFunctionType
AX_X = mybir.AxisListType.X

P = 128
D = 1024
KD = D // P
CTX, SEQ = 256, 256
TOK = CTX + SEQ
TT = SEQ // P
DEPTH = 2
HEADS, DK, DV = 4, 64, 128
RT = HEADS * DK // P
RANK = 16
CHUNK = 64
NCH = TOK // CHUNK
NG = TOK // P
GATE_NORM = 16.0
EPS = 1e-6
DFF = 2816
JF = DFF // P
NE = 8
DFE = 3584
JE = DFE // P
LEVELS = [32, 16, 8, 4, 2, 1]
COL = {"qk": 0, "v": 512, "g": 1024, "a": 1536, "B": 1568, "C": 2080, "h": 2592}

BM, GMP, GMO, GFP, GFO, BD, GN, CW, CC, CX = 0, 48, 56, 64, 72, 80, 84, 85, 97, 105
VROWS = 113

MODS = {"start": (0, 1, 2, 3), "keys": (9, 10, 11), "added": (0, 1, 2), "states": (3, 4, 5), "outputs": (6, 7, 8),
        "residual": (9, 10, 11)}

SLOTS = 5
CHUNKW = KD * 512
ESLOTS = 7
PIECE = 3 * D
WIDTHS = (64, 128, 256)
BODY = 14
UNITS = 2 * JF
MISC = 14


def by_width(eng, chosen, body):
    with eng.If(chosen > WIDTHS[1]):
        body(WIDTHS[2])
    with eng.If(chosen < WIDTHS[1] + 1):
        with eng.If(chosen > WIDTHS[0]):
            body(WIDTHS[1])
        with eng.If(chosen < WIDTHS[0] + 1):
            body(WIDTHS[0])


def plan():
    uses = []
    turn = [0]

    def use(name, bank, *chunks):
        uses.append((name, bank, chunks))

    def rot():
        turn[0] += 1
        return (turn[0] - 1) % 4

    def mods(layer, chunks, banks=None):
        at = [0]

        def nxt():
            at[0] += 1
            return rot() if banks is None else banks[(at[0] - 1) % len(banks)]

        for n, i in enumerate(chunks):
            use(("mrow", layer, i), nxt(), ("mod", layer, i))
            if n:
                use(("mcol", layer, chunks[n - 1]), nxt())
        use(("mcol", layer, chunks[-1]), nxt())

    for k in range(KD):
        use(("xt", k), rot())
    use(("vec", 0), 6)
    mods(0, MODS["start"])
    use(("vec", 1), 7)
    for L in range(DEPTH):
        blocks = range(4) if L == 0 else range(2, 4)
        use(("ssq", 2 * L), 4)
        for m in range(RT):
            use(("q", L, m), rot(), ("qk", L))
        for m in range(RT):
            use(("k", L, m), rot(), ("qk", L))
        use(("a", L), rot(), ("a", L))
        for i in range(4):
            use(("z", L, i), rot())
        for g in range(NG):
            use(("v", L, g), rot(), ("v", L))
        for b in blocks:
            use(("P", L, 0, b), 4 + b)
        for s in range(len(LEVELS)):
            if L == 0 and s < 5:
                use(("mrow", 0, 4 + s), rot(), ("mod", 0, 4 + s))
            if s < 2:
                use(("g", L, 2 * s), rot(), ("g", L))
                use(("g", L, 2 * s + 1), rot(), ("g", L))
            else:
                for w in "ChB":
                    use((w, L, s - 2), rot(), (w, L))
            if L == 0 and s < 5:
                use(("mcol", 0, 4 + s), rot())
            for b in blocks:
                use(("P", L, s + 1, b), 4 + b)
        if L == 0:
            mods(0, MODS["keys"])
        for i in range(4):
            use(("kt", L, i), 4 + i)
        if L == 0:
            mods(1, MODS["added"])
        for i in range(4):
            use(("U", L, 0, i), rot())
        for i in range(4):
            use(("U", L, 1, i), 4 + i)
        if L == 0:
            mods(1, MODS["states"])
        for h in range(HEADS):
            use(("o", L, h), rot())
        if L == 0:
            mods(1, MODS["outputs"], (4, 5, 6, 7))
        for h in range(HEADS):
            use(("oss", L, h), 4 + h)
        for m in range(KD):
            use(("y", L, m), rot(), ("wo", L, m // 4))
        use(("yss", 2 * L), 4)
        if L == 0:
            mods(1, MODS["residual"], (6, 7))
        use(("ssq", 2 * L + 1), 5)
        if L == 0:
            for j in range(JF):
                use(("ffg", j), rot(), ("ff", j // 2))
                use(("ffu", j), rot(), ("ff", j // 2))
            for half in range(2):
                for m in range(4):
                    use(("y2", 4 * half + m), 4 + m if half == 0 else rot(), *[("w2", half, i) for i in range(3)])
            use(("yss", 1), 4)
    use(("lg",), 6)
    for i in range(4):
        use(("ht", i), rot())
    use(("pos",), 7)
    use(("yss", 3), 4)
    for i in range(4):
        use(("out", i), rot())
    return uses


def hybrid_backbone(nc, x, c, ctx_in, c_ctx, w_mod, b_mod, g_mix_pre, g_mix_post, w_in, w_decay, b_decay, gla_norm,
                    conv_w, w_out, g_ffn_pre, g_ffn_post, w1, w3, w2, w_router, e_w1, e_w3, e_w2, out):
    uses = plan()
    tile_at, bank_of, nth_of = {}, {}, {}
    chunk_order, chunk_last = [], {}
    count = [0] * 8
    for n, (name, bank, chunks) in enumerate(uses):
        tile_at[name], bank_of[name], nth_of[name] = n, bank, count[bank]
        count[bank] += 1
        for ch in chunks:
            if ch not in chunk_last:
                chunk_order.append(ch)
            chunk_last[ch] = n
    chunk_at = {ch: i for i, ch in enumerate(chunk_order)}
    slot_sum = [0] * SLOTS
    chunk_value = {}
    for i, ch in enumerate(chunk_order):
        slot_sum[i % SLOTS] += 32 if ch[0] == "ff" else 16
        chunk_value[ch] = slot_sum[i % SLOTS]

    sums = [(name, 1 if name[0] == "oss" else KD) for name, _, _ in uses if name[0] in ("ssq", "oss", "yss")]

    with ExitStack() as stack:
        def sb(name, shape, dt=F32):
            return stack.enter_context(nc.sbuf_tensor(name, shape, dt))

        def sem(name):
            return stack.enter_context(nc.semaphore(name))

        def sb_twice(name, shape):
            with nc.sbuf_tensor(name + "_rounded", shape, F32R) as rounded:
                pass
            return sb(name, shape), rounded

        ring, ring_r = sb_twice("ring", [P, ESLOTS * PIECE])
        xT = sb("xT", [P, KD, TOK])
        hT, x_low = sb_twice("hT", [P, KD, TOK])
        mixT, x_high = sb_twice("mixT", [P, KD, TOK])
        with nc.sbuf_tensor("below_rounded", [P, JF * TOK], F32):
            with nc.sbuf_tensor("work_rounded", [P, 14336 - JF * TOK], F32R) as work_r:
                pass
        work = sb("work", [P, 14336])
        sq = sb("sq", [P, 2, TOK])
        rs = sb("rs", [P, 2, TOK])
        tmp = sb("tmp", [P, 2, TOK])
        ident = sb("ident", [P, P])
        ones = sb("ones", [P, P])
        masks = sb("masks", [P, len(LEVELS), P], U8)
        first0 = sb("first0", [P, TOK], U8)
        last0 = sb("last0", [P, TOK], U8)
        vecs = sb("vecs", [P, DEPTH, VROWS])
        modv = sb("modv", [P, DEPTH, 6, KD, 2])
        csil = sb("csil", [P, KD, 32])
        rank_rows = sb("rank_rows", [2 * RANK, 2])
        dec = sb("dec", [P, 2, RT, NCH])
        wr = sb("wr", [P, KD, NE])
        small = sb("small", [P, 16, NE])
        cnt_i = sb("cnt_i", [1, NE], I32)
        eps = sb("eps", [P, 1])
        one = sb("one", [P, 1])
        ps = [stack.enter_context(nc.psum_tensor(f"ps{i}", [P, 512], F32)) for i in range(8)]

        def part(at, *dims, of=work):
            n = int(np.prod(dims))
            a = of[:, at:at + n]
            if len(dims) == 2:
                a = a.rearrange("p (a b) -> p a b", a=dims[0])
            if len(dims) == 3:
                a = a.rearrange("p (a b c) -> p a b c", a=dims[0], b=dims[1])
            if len(dims) == 4:
                a = a.rearrange("p (a b c d) -> p a b c d", a=dims[0], b=dims[1], c=dims[2])
            return a

        mrow = ring[:, SLOTS * CHUNKW:SLOTS * CHUNKW + 512]
        wdec = ring[0:2 * RANK, SLOTS * CHUNKW + 512:SLOTS * CHUNKW + 1024].rearrange("p (l n) -> p l n", l=DEPTH)
        qT = part(0, RT, TOK)
        kT = part(1024, RT, TOK)
        vtok = part(2048, NG, HEADS * DV)
        la = part(4096, 2, RT, TOK)
        kdt = part(4096, 2, NG, HEADS * DK)
        cum = part(6144, 2, RT, TOK)
        lvl = part(8192, 2, 2, RT, TOK)
        att = part(12288, 4, 4, P)
        a2 = work[0:2 * RANK, 12288:12288 + 2 * TOK].rearrange("p (a b) -> p a b", a=2)
        states = hT[:, :, :].rearrange("p a b -> p (a b)").rearrange("p (d c r v) -> p d c r v", d=2, c=NCH, r=RT)
        ffh = part(0, JF, TOK)
        w_high = part(0, 3, KD, P, of=work_r)
        w2_high = part(0, 2, 512, of=work_r)
        ff_high = part(1024, 2, TOK, of=work_r)
        ff_low = part(2048, 2, TOK, of=work_r)
        htok = part(0, TT, D)
        xsel = part(2048, KD, 256)
        ye = part(4096, KD, 256)
        raw = part(4096, 2, P)
        yhalf = part(6144, 512)
        yslot = part(6144, 2, D)
        swt = part(8192, 2, SEQ)
        selg = part(8704, TT, 256)
        selw = part(9216, TT, 256)
        yacc = part(9728, KD, SEQ)
        esg = part(11776, 2, 256)
        eh = part(12288, 2, 256)
        slotno = part(12800, 256)
        before = part(13056, P)
        tie = part(13184, NE * NE)
        route = part(13568, 2, NE * NE)
        zeros = work[:, 13312:13312 + 256].bitcast(BF16)
        vrow = part(0, DEPTH, P)
        xrow = mixT[:, :, :].rearrange("p a b -> p (a b)").rearrange("p (t d) -> p t d", t=NG)
        iota_i = work[:, 1024:1024 + P].bitcast(I32)
        iota_j = work[:, 1152:1152 + P].bitcast(I32)
        ixor = work[:, 1280:1280 + P].bitcast(I32)
        iota_t = work[:, 1408:1408 + TOK].bitcast(I32)
        iota_r = work[0:2 * RANK, 1920:1921].bitcast(I32)
        itmp = work[:, 2048:2048 + P]
        iota_s = work[:, 11776:11776 + 256].bitcast(I32)
        iota_b = work[:, 12032:12032 + P].bitcast(I32)
        iota_e = work[:, 12160:12160 + NE * NE].bitcast(I32)
        osb = hT[:, :, :].rearrange("p a b -> p (a b)").rearrange("p (t d) -> p t d", t=NG)

        def slot(name, of=ring):
            i = chunk_at[name] % SLOTS
            return of[:, i * CHUNKW:(i + 1) * CHUNKW]

        tile_ready = sem("tile_ready")
        mod_order = [name[1:] for name, _, _ in uses if name[0] == "mrow"]
        drained = [sem(f"bank{i}_drained") for i in range(8)]
        chunk_in = [sem(f"chunk_in{i}") for i in range(SLOTS)]
        rows_in = sem("rows_in")
        consts_in = [sem(f"consts_in{i}") for i in range(DEPTH)]
        router_in = sem("router_in")
        vrow_clear = sem("vrow_clear")
        iota_done = sem("iota_done")
        consts_done = sem("consts_done")
        csil_ready = sem("csil_ready")
        sq_ready = sem("sq_ready")
        sq_used = sem("sq_used")
        rs_ready = sem("inverse_rms_ready")
        rs_used = sem("rs_used")
        mod_ready = sem("mod_ready")
        h_ready = sem("h_ready")
        res_ready = sem("res_ready")
        lnz_ready = sem("lnz_ready")
        cum_ready = sem("cum_ready")
        diff_ready = sem("diff_ready")
        decay_ready = sem("decay_ready")
        level_ready = sem("level_ready")
        state_diff = sem("state_diff")
        state_exp = sem("state_exp")
        state_ops = sem("state_ops")
        states_ready = sem("states_ready")
        conv_read = sem("conv_read")
        gate_ready = sem("gate_ready")
        mix_ready = sem("mix_ready")
        sg_ready = sem("sg_ready")
        vstep = sem("vector_step")
        astep = sem("scalar_step")
        ex_ready = sem("expert_exp")
        logits_in = sem("logits_in")
        sel_counted = sem("selection_ready")
        route_ready = sem("route_ready")
        iota2_done = sem("iota2_done")
        consts2_done = sem("consts2_done")
        piece_in = [sem(f"piece_in{i}") for i in range(ESLOTS)]
        piece_free = [sem(f"piece_free{i}") for i in range(ESLOTS)]
        sel_ready = sem("sel_ready")
        misc_ready = sem("misc_ready")
        misc_drained = sem("misc_drained")
        y_drained = sem("y_drained")
        raw_ready = sem("raw_ready")
        raw_copied = sem("raw_copied")
        gu_ready = sem("gu_ready")
        gu_drained = sem("gu_drained")
        esg_ready = sem("esg_ready")
        x_split = sem("x_split")
        w_split = sem("w_split")
        w2_split = sem("w2_split")
        w2_used = sem("w2_used")
        stored = sem("stored")

        sq_free, rs_free = [], []
        passed = [0, 0]
        for name, tiles in sums:
            for k in range(tiles - 1):
                passed[0] += 1
                sq_free.append((sq_used, passed[0]))
            sq_free.append((tile_ready, tile_at[name] + 1))
            if name[0] == "oss":
                o = ("o", *name[1:])
                rs_free.append((drained[bank_of[o]], nth_of[o] + 1))
            else:
                passed[1] += 1
                rs_free.append((rs_used, passed[1]))

        block = stack.enter_context(nc.Block())

        def wait_tile(eng, name):
            eng.wait_ge(tile_ready, tile_at[name] + 1)

        def wait_drained(eng, name):
            eng.wait_ge(drained[bank_of[name]], nth_of[name] + 1)

        def drains(ins, name):
            ins.then_inc(drained[bank_of[name]], 1)

        def bank(name):
            return ps[bank_of[name]]

        def first_col(L):
            return 0 if L == 0 else CTX

        def unit_weights(u, of=ring):
            j = u // 2
            w = slot(("ff", j // 2), of).rearrange("p (w k n) -> p w k n", w=2, k=KD)
            return w[:, u % 2, :, (j % 2) * P:(j % 2 + 1) * P]

        def unit_tile(u):
            return ("ffu" if u % 2 else "ffg", u // 2)

        def rows(w, a, n):
            return w[:, a:a + n].rearrange("(k p) n -> p k n", p=P)

        @block.sync
        def _(sp):
            for t in range(NG):
                src = ctx_in[0] if t < 2 else x[0]
                sp.dma_start(xrow[:, t, :], src[(t % 2) * P:(t % 2 + 1) * P, :]).then_inc(rows_in, 16)
            sp.wait_ge(consts_in[0], 16 * 11)
            for i, ch in enumerate(chunk_order):
                if i >= SLOTS:
                    sp.wait_ge(tile_ready, chunk_last[chunk_order[i - SLOTS]] + 1)
                kind = ch[0]
                dst = slot(ch)
                full = chunk_in[i % SLOTS]
                d3 = dst.rearrange("p (k n) -> p k n", k=KD)
                if kind == "mod":
                    sp.dma_start(d3, rows(w_mod[ch[1]], 512 * ch[2], 512)).then_inc(full, 16)
                elif kind == "a":
                    sp.dma_start(d3[:, :, 0:2 * RANK], rows(w_in[ch[1]], COL["a"], 2 * RANK)).then_inc(full, 16)
                elif kind in COL:
                    sp.dma_start(d3, rows(w_in[ch[1]], COL[kind], 512)).then_inc(full, 16)
                elif kind == "wo":
                    sp.dma_start(d3, rows(w_out[ch[1]], 512 * ch[2], 512)).then_inc(full, 16)
                elif kind == "ff":
                    d4 = dst.rearrange("p (w k n) -> p w k n", w=2, k=KD)
                    sp.dma_start(d4[:, 0], rows(w1[0], 256 * ch[1], 256)).then_inc(full, 16)
                    sp.dma_start(d4[:, 1], rows(w3[0], 256 * ch[1], 256)).then_inc(full, 16)
                else:
                    k0 = 8 * ch[2]
                    nk = min(8, JF - k0)
                    src = rows(w2[0][k0 * P:(k0 + nk) * P], 512 * ch[1], 512)
                    sp.dma_start(d3[:, 0:nk], src).then_inc(full, 16)
            sp.wait_ge(tile_ready, chunk_last[chunk_order[-1]] + 1)
            for s in range(ESLOTS):
                sp.sem_inc(piece_free[s], 1)
            with sp.Fori(0, NE) as e:
                with sp.Fori(0, JE // ESLOTS) as r:
                    for s in range(ESLOTS):
                        sp.wait_ge(piece_free[s], e * (JE // ESLOTS) + r + 1)
                        dst = ring[:, s * PIECE:(s + 1) * PIECE]
                        cols = bass.ds(r * (ESLOTS * P) + s * P, P)
                        for w, src in ((0, e_w1), (1, e_w3)):
                            sp.dma_start(
                                dst[:, w * D:(w + 1) * D].rearrange("p (k n) -> p k n", k=KD),
                                src[0, bass.ds(e, 1), :, cols].rearrange("a (k p) n -> p (a k) n", p=P),
                            ).then_inc(piece_in[s], 16)
                        sp.dma_start(dst[:, 2 * D:3 * D],
                                     e_w2[0, bass.ds(e, 1), cols, :].rearrange("a p n -> p (a n)"),
                                     ).then_inc(piece_in[s], 16)
            for i in range(4):
                wait_drained(sp, ("out", i))
                sp.dma_start(out[0, (i // 2) * P:(i // 2 + 1) * P, (i % 2) * 512:(i % 2 + 1) * 512],
                             osb[:, i // 2, (i % 2) * 512:(i % 2 + 1) * 512]).then_inc(stored, 16)
            sp.wait_ge(stored, 64)

        @block.gpsimd
        def _(pool):
            pool.memset(vrow, 0.0).then_inc(vrow_clear, 1)
            pool.iota(iota_i, pattern=[[1, P]], base=0, channel_multiplier=0).then_inc(iota_done, 1)
            pool.iota(iota_j, pattern=[[0, P]], base=0, channel_multiplier=1).then_inc(iota_done, 1)
            pool.iota(iota_t, pattern=[[0, NCH], [1, CHUNK]], base=0, channel_multiplier=0).then_inc(iota_done, 1)
            pool.iota(iota_r, pattern=[[1, 1]], base=0, channel_multiplier=1).then_inc(iota_done, 1)
            wait_drained(pool, ("y", DEPTH - 1, 0))
            pool.iota(iota_s, pattern=[[1, 256]], base=0, channel_multiplier=0).then_inc(iota2_done, 1)
            pool.iota(iota_b, pattern=[[1, P]], base=0, channel_multiplier=-1).then_inc(iota2_done, 1)
            pool.iota(iota_e, pattern=[[1, NE], [-1, NE]], base=0, channel_multiplier=0).then_inc(iota2_done, 1)

        @block.tensor
        def _(pe):
            at = [0]

            def begin(name):
                assert tile_at[name] == at[0], name
                if nth_of[name]:
                    pe.wait_ge(drained[bank_of[name]], nth_of[name])
                return bank(name)

            def end(ins):
                ins.then_inc(tile_ready, 1)
                at[0] += 1

            def weights(ch, **dims):
                pe.wait_ge(chunk_in[chunk_at[ch] % SLOTS], chunk_value[ch])
                if not dims:
                    dims = {"k": KD}
                names = " ".join(dims)
                return slot(ch).rearrange(f"p ({names} n) -> p {names} n", **dims)

            nsq = [0]

            def add_square(name, k, tiles, n):
                if k == 0 and nth_of[name]:
                    pe.wait_ge(drained[bank_of[name]], nth_of[name])
                pe.wait_ge(sq_ready, nsq[0] + 1)
                ins = pe.matmul(bank(name)[:, 0:n], ones[:], sq[:, nsq[0] % 2, 0:n],
                                start=(k == 0), stop=(k == tiles - 1))
                if k < tiles - 1:
                    ins.then_inc(sq_used, 1)
                else:
                    assert tile_at[name] == at[0], name
                    end(ins)
                nsq[0] += 1

            def square_sum(name, tiles, n):
                for k in range(tiles):
                    add_square(name, k, tiles, n)

            def mod_rows(layer, i):
                acc = begin(("mrow", layer, i))
                w = weights(("mod", layer, i))
                for kk in range(2):
                    for g in range(4):
                        k = 4 * kk + g
                        ins = pe.matmul(acc[32 * g:32 * g + 32, :], csil[:, k, :], w[:, k, :],
                                        start=(kk == 0), stop=(kk == 1), skip_group_check=True)
                end(ins)

            def mod_cols(layer, i):
                acc = begin(("mcol", layer, i))
                wait_drained(pe, ("mrow", layer, i))
                for m in range(4):
                    ins = pe.transpose(acc[:, m * P:(m + 1) * P], mrow[:, m * P:(m + 1) * P], ident[:])
                end(ins)

            def mods(layer, chunks):
                for n, i in enumerate(chunks):
                    mod_rows(layer, i)
                    if n:
                        mod_cols(layer, chunks[n - 1])
                mod_cols(layer, chunks[-1])

            def project(name, w, m, c0, norm, width=P):
                acc = begin(name)
                for k in range(KD):
                    pe.wait_ge(h_ready, norm * KD + k + 1)
                    ins = pe.matmul(acc[0:width, 0:TOK - c0], w[:, k, m * P:m * P + width], hT[:, k, c0:],
                                    start=(k == 0), stop=(k == KD - 1))
                end(ins)

            def product(acc, w_high_, w_low_, x_high_, x_low_, first, last):
                pe.matmul(acc, w_high_, x_high_, start=first, stop=False)
                pe.matmul(acc, w_high_, x_low_, start=False, stop=False)
                return pe.matmul(acc, w_low_, x_high_, start=False, stop=last)

            def vectors(L):
                pe.wait_ge(consts_in[L], 16 * 11)
                acc = begin(("vec", L))
                end(pe.transpose(acc[:, 0:VROWS], vrow[0:VROWS, L, :], ident[0:VROWS, 0:VROWS]))

            pe.wait_ge(consts_done, 1)
            pe.wait_ge(rows_in, 16 * NG)
            for k in range(KD):
                acc = begin(("xt", k))
                for t in range(NG):
                    ins = pe.transpose(acc[:, t * P:(t + 1) * P], xrow[:, t, k * P:(k + 1) * P], ident[:])
                end(ins)
            vectors(0)
            pe.wait_ge(csil_ready, 2)
            mods(0, MODS["start"])
            vectors(1)
            pe.wait_ge(router_in, 16)

            for L in range(DEPTH):
                c0 = first_col(L)
                n = TOK - c0
                groups = range(c0 // P, NG)
                square_sum(("ssq", 2 * L), KD, TOK)
                w = weights(("qk", L))
                for m in range(RT):
                    project(("q", L, m), w, m, c0, 2 * L)
                for m in range(RT):
                    project(("k", L, m), w, RT + m, 0, 2 * L)
                project(("a", L), weights(("a", L)), 0, 0, 2 * L, width=2 * RANK)
                wait_drained(pe, ("a", L))
                for i in range(4):
                    acc = begin(("z", L, i))
                    end(pe.matmul(acc[:], wdec[:, L, (i % 2) * P:(i % 2 + 1) * P], a2[:, i // 2, :],
                                  start=True, stop=True))
                w = weights(("v", L))
                for g in range(NG):
                    acc = begin(("v", L, g))
                    for k in range(KD):
                        ins = pe.matmul(acc[:], hT[:, k, g * P:(g + 1) * P], w[:, k, :],
                                        start=(k == 0), stop=(k == KD - 1))
                    end(ins)

                def scores(s, key, query):
                    for b in range(c0 // P, 4):
                        acc = begin(("P", L, s, b))
                        for gi in range(2):
                            for r in range(RT):
                                rows_ = slice(DK * (b % 2), DK * (b % 2) + DK)
                                g = 2 * (b // 2) + gi
                                o = (2 * gi + r) * P
                                ins = pe.matmul(acc[:, o:o + P], key[rows_, r, g * P:(g + 1) * P],
                                                query[rows_, r, g * P:(g + 1) * P], start=True, stop=True)
                        end(ins)

                scores(0, kT, qT)
                for s in range(len(LEVELS)):
                    if L == 0 and s < 5:
                        mod_rows(0, 4 + s)
                    if s < 2:
                        for m in (2 * s, 2 * s + 1):
                            project(("g", L, m), weights(("g", L)), m, c0, 2 * L)
                    else:
                        for kind in "ChB":
                            project((kind, L, s - 2), weights((kind, L)), s - 2, c0, 2 * L)
                    if L == 0 and s < 5:
                        mod_cols(0, 4 + s)
                    pe.wait_ge(level_ready, 2 * (len(LEVELS) * L + s + 1))
                    scores(s + 1, lvl[:, s % 2, 1], lvl[:, s % 2, 0])
                if L == 0:
                    mods(0, MODS["keys"])
                pe.wait_ge(state_ops, 4 * L + 2)
                for i in range(4):
                    acc = begin(("kt", L, i))
                    for gi in range(2):
                        for r in range(RT):
                            g = 2 * (i % 2) + gi
                            o = (2 * gi + r) * P
                            ins = pe.transpose(acc[:, o:o + P], lvl[:, 0, i // 2, r, g * P:(g + 1) * P], ident[:])
                    end(ins)
                if L == 0:
                    mods(1, MODS["added"])
                for d in range(2):
                    for i in range(4):
                        wait_drained(pe, ("kt", L, 2 * d + (i // 2)))
                        acc = begin(("U", L, d, i))
                        for j in range(2):
                            ch = 4 * (i // 2) + i % 2 + 2 * j
                            g, base = ch // 2, CHUNK * (ch % 2)
                            for r in range(RT):
                                for p in range(2):
                                    h = 2 * r + p
                                    ins = pe.matmul(
                                        acc[DK * p:DK * p + DK, (2 * j + r) * DV:(2 * j + r + 1) * DV],
                                        kdt[base:base + CHUNK, d, g, h * DK:(h + 1) * DK],
                                        vtok[base:base + CHUNK, g, h * DV:(h + 1) * DV], start=True, stop=True)
                        end(ins)
                if L == 0:
                    mods(1, MODS["states"])
                for b in range(c0 // P, 4):
                    wait_drained(pe, ("P", L, len(LEVELS), b))
                pe.wait_ge(states_ready, L + 1)
                pe.wait_ge(state_ops, 4 * L + 4)
                for h in range(HEADS):
                    acc = begin(("o", L, h))
                    p, r = h % 2, h // 2
                    rows_ = slice(DK * p, DK * p + DK)
                    for g in groups:
                        b = 2 * (g // 2) + p
                        pe.matmul(acc[:, g * P - c0:(g + 1) * P - c0], vtok[:, g, h * DV:(h + 1) * DV],
                                  att[:, b, 2 * (g % 2) + r, :], start=True, stop=False, skip_group_check=True)
                        for d in range(2):
                            for ch in (2 * g, 2 * g + 1):
                                if (d == 0 and ch == 0) or (d == 1 and ch == NCH // 2 - 1):
                                    continue
                                o = ch * CHUNK
                                ins = pe.matmul(acc[:, o - c0:o - c0 + CHUNK], states[rows_, d, ch, r, :],
                                                lvl[rows_, 1, d, r, o:o + CHUNK], start=False, stop=True,
                                                skip_group_check=True)
                    end(ins)
                if L == 0:
                    mods(1, MODS["outputs"])
                for h in range(HEADS):
                    square_sum(("oss", L, h), 1, n)
                for m in range(KD):
                    w = weights(("wo", L, m // 4))
                    acc = begin(("y", L, m))
                    for i, k in enumerate((4, 5, 6, 7, 0, 1, 2, 3)):
                        if k < HEADS:
                            pe.wait_ge(mix_ready, HEADS * L + k + 1)
                        else:
                            wait_drained(pe, ("B", L, k - HEADS))
                        ins = pe.matmul(acc[:, 0:n], w[:, k, (m % 4) * P:(m % 4 + 1) * P], mixT[:, k, c0:],
                                        start=(i == 0), stop=(i == KD - 1))
                    end(ins)
                    if m:
                        add_square(("yss", 2 * L), m - 1, KD, n)
                add_square(("yss", 2 * L), KD - 1, KD, n)
                if L == 0:
                    mods(1, MODS["residual"])
                square_sum(("ssq", 2 * L + 1), KD, n)
                if L == 0:
                    for u in range(UNITS):
                        acc = begin(unit_tile(u))
                        pe.wait_ge(w_split, u + 1)
                        high, low = w_high[:, u % 3], unit_weights(u, ring_r)
                        for k in range(KD):
                            if u == 0:
                                pe.wait_ge(x_split, k + 1)
                            ins = product(acc[:], high[:, k, :], low[:, k, :], x_high[:, k, :], x_low[:, k, :],
                                          k == 0, k == KD - 1)
                        end(ins)
                    for half in range(2):
                        accs = []
                        for m in range(4):
                            name = ("y2", 4 * half + m)
                            pe.wait_ge(drained[bank_of[name]], nth_of[name])
                            accs.append(bank(name))
                        for i in range(3):
                            w = slot(("w2", half, i), ring_r).rearrange("p (k n) -> p k n", k=KD)
                            for k in range(8 * i, min(8 * i + 8, JF)):
                                d = half * JF + k
                                pe.wait_ge(w2_split, 2 * d + 2)
                                for m in range(4):
                                    cols = slice(m * P, (m + 1) * P)
                                    ins = product(accs[m][:], w2_high[:, d % 2, cols], w[:, k - 8 * i, cols],
                                                  ff_high[:, d % 2, :], ff_low[:, d % 2, :],
                                                  k == 0, k == JF - 1)
                                    if k == JF - 1:
                                        end(ins)
                                if k < JF - 1:
                                    ins.then_inc(w2_used, 1)
                            if half == 1 and i == 0:
                                for m in range(4):
                                    add_square(("yss", 1), m, KD, TOK)
                    for m in range(4, KD):
                        add_square(("yss", 1), m, KD, TOK)

            acc = begin(("lg",))
            for t in range(TT):
                for k in range(KD):
                    pe.wait_ge(h_ready, 3 * KD + k + 1)
                    ins = pe.matmul(acc[:, t * NE:(t + 1) * NE], hT[:, k, CTX + t * P:CTX + (t + 1) * P], wr[:, k, :],
                                    start=(k == 0), stop=(k == KD - 1))
            end(ins)
            for i in range(4):
                acc = begin(("ht", i))
                for j in range(4):
                    k = 4 * (i % 2) + j
                    o = CTX + (i // 2) * P
                    ins = pe.transpose(acc[:, j * P:(j + 1) * P], hT[:, k, o:o + P], ident[:])
                end(ins)
            pe.wait_ge(sel_counted, 1)
            pe.wait_ge(consts2_done, 3)
            sel = small[:, 0:2, :]
            acc = begin(("pos",))
            pe.matmul(acc[:, 0:NE], before, sel[:, 0, :], start=True, stop=True)
            pe.matmul(acc[:, NE:2 * NE], ones[:], sel[:, 0, :], start=True, stop=False)
            pe.matmul(acc[:, NE:2 * NE], before, sel[:, 1, :], start=False, stop=True)
            pe.matmul(acc[:, 2 * NE:3 * NE], ones[:], sel[:, 0, :], start=True, stop=False)
            end(pe.matmul(acc[:, 2 * NE:3 * NE], ones[:], sel[:, 1, :], start=False, stop=True))
            for b in range(8):
                pe.wait_ge(drained[b], max(nth_of[n] for n in tile_at if bank_of[n] == b and tile_at[n] < at[0]) + 1)
            pe.wait_ge(route_ready, 1)

            def spare(e, i):
                pe.wait_ge(misc_drained, e * MISC + (i + 1))
                return ps[6 + i % 2]

            def piece_arrived(e, q, j):
                pe.wait_ge(piece_in[j % ESLOTS], e * (48 * JE // ESLOTS) + q * (48 * BODY // ESLOTS)
                           + 48 * (j // ESLOTS + 1))

            def gather(e, W):
                sh_n = (W + P - 1) // P
                pe.wait_ge(sel_ready, e * 4 + 4)
                for i in range(4):
                    acc = spare(e, i)
                    for m in (2 * i, 2 * i + 1):
                        o = (m % 2) * 256
                        for t in range(TT):
                            ins = pe.matmul(acc[:, o:o + W], htok[:, t, m * P:(m + 1) * P], selg[:, t, 0:W],
                                            start=(t == 0), stop=(t == TT - 1))
                    ins.then_inc(misc_ready, 1)
                for t in range(TT):
                    acc = spare(e, 4 + t)
                    for s in range(sh_n):
                        ins = pe.transpose(acc[:, s * P:(s + 1) * P], selw[:, t, s * P:(s + 1) * P], ident[:])
                    ins.then_inc(misc_ready, 1)
                pe.wait_ge(misc_drained, e * MISC + (4 + 2))

            def few(e):
                gather(e, P)
                H = WIDTHS[0]
                pe.wait_ge(y_drained, e * 4 + 1)
                pe.matmul(ps[0][:], zeros[:, 0:P], zeros, start=True, stop=True, skip_group_check=True)

                with pe.Fori(0, JE // BODY) as q:
                    def slot_major(j):
                        piece_arrived(e, q, j)
                        pe.wait_ge(raw_copied, e * JE + q * BODY + (j + 1))
                        at_ = (j % ESLOTS) * PIECE
                        for k in range(KD):
                            for w in range(2):
                                o = at_ + w * D + k * P
                                ins = pe.matmul(ps[2 + j % 2][H * w:H * w + H, 0:P], xsel[:, k, 0:H],
                                                ring[:, o:o + P], start=(k == 0), stop=(k == KD - 1),
                                                skip_group_check=True)
                        ins.then_inc(raw_ready, 1)

                    def turn(j):
                        pe.wait_ge(gu_drained, e * JE + q * BODY + (j + 1))
                        pe.wait_ge(raw_copied, e * JE + q * BODY + (j + 3))
                        pe.transpose(ps[4 + j % 2][:, 0:P], raw[:, j % 2, :], ident[:]).then_inc(gu_ready, 1)

                    def down(j):
                        pe.wait_ge(gu_drained, e * JE + q * BODY + (j + 3))
                        at_ = (j % ESLOTS) * PIECE + 2 * D
                        for half in range(2):
                            ins = pe.matmul(ps[0][H * half:H * half + H, :], eh[:, j % 2, 0:H],
                                            ring[:, at_ + 512 * half:at_ + 512 * half + 512],
                                            start=False, stop=True, skip_group_check=True)
                        ins.then_inc(piece_free[j % ESLOTS], 1)

                    for j in range(BODY + 2):
                        if j < BODY:
                            slot_major(j)
                        if 1 <= j <= BODY:
                            turn(j - 1)
                        if j >= 2:
                            down(j - 2)

                pe.sem_inc(misc_ready, 4)
                pe.wait_ge(y_drained, e * 4 + 5)
                for i in range(4):
                    acc = spare(e, 10 + i)
                    rows_ = slice(H * (i // 2), H * (i // 2) + H)
                    for mi in range(2):
                        o = (2 * (i % 2) + mi) * P
                        ins = pe.matmul(acc[:, mi * 256:(mi + 1) * 256], yhalf[rows_, o:o + P], swt[rows_, 0, :],
                                        start=True, stop=True)
                    ins.then_inc(misc_ready, 1)

            def expert(e, W):
                if W == WIDTHS[0]:
                    return few(e)
                sh_n = (W + P - 1) // P
                wp = min(W, P)
                pe.sem_inc(raw_ready, JE)
                gather(e, W)
                pe.wait_ge(y_drained, e * 4 + 1)
                for b in range(4):
                    pe.matmul(ps[b][:], zeros[:, 0:P], zeros, start=True, stop=True, skip_group_check=True)
                with pe.Fori(0, JE // BODY) as q:
                    def hidden(j):
                        s = j % ESLOTS
                        piece_arrived(e, q, j)
                        pe.wait_ge(gu_drained, e * JE + q * BODY + (j + 1))
                        acc = ps[4 + j % 2]
                        for w in range(2):
                            piece = ring[:, s * PIECE + w * D:s * PIECE + (w + 1) * D]
                            for k in range(KD):
                                ins = pe.matmul(acc[:, 256 * w:256 * w + W], piece[:, k * P:(k + 1) * P],
                                                xsel[:, k, 0:W], start=(k == 0), stop=(k == KD - 1))
                        ins.then_inc(gu_ready, 1)

                    def down(j):
                        s = j % ESLOTS
                        pe.wait_ge(gu_drained, e * JE + q * BODY + (j + 3))
                        piece = ring[:, s * PIECE + 2 * D:s * PIECE + 3 * D]
                        for m in range(KD):
                            o = (m % 2) * 256
                            ins = pe.matmul(ps[m // 2][:, o:o + W], piece[:, m * P:(m + 1) * P], eh[:, j % 2, 0:W],
                                            start=False, stop=True, skip_group_check=True)
                        ins.then_inc(piece_free[s], 1)

                    hidden(0)
                    for j in range(1, BODY):
                        hidden(j)
                        down(j - 1)
                    down(BODY - 1)

                pe.wait_ge(y_drained, e * 4 + 5)
                for i in range(4):
                    acc = spare(e, 6 + i)
                    for s in range(sh_n):
                        for mi in range(2):
                            ins = pe.transpose(acc[:, s * 256 + mi * P:s * 256 + (mi + 1) * P],
                                               ye[:, 2 * i + mi, s * P:(s + 1) * P], ident[:])
                    ins.then_inc(misc_ready, 1)
                for i in range(4):
                    acc = spare(e, 10 + i)
                    pe.wait_ge(misc_drained, e * MISC + (6 + i + 3))
                    for mi in range(2):
                        m = 2 * i + mi
                        for s in range(sh_n):
                            ins = pe.matmul(acc[:, mi * 256:(mi + 1) * 256], yslot[0:wp, s, m * P:(m + 1) * P],
                                            swt[0:wp, s, :], start=(s == 0), stop=(s == sh_n - 1))
                    ins.then_inc(misc_ready, 1)

            with pe.Fori(0, NE) as e:
                chosen = pe.value_load(cnt_i[0:1, bass.ds(e, 1)], min_val=0, max_val=SEQ)
                by_width(pe, chosen, lambda W: expert(e, W))

            pe.wait_ge(misc_drained, NE * MISC + 2)
            square_sum(("yss", 3), KD, SEQ)
            for i in range(4):
                acc = begin(("out", i))
                for j in range(4):
                    k = 4 * (i % 2) + j
                    pe.wait_ge(res_ready, 3 * KD + k + 1)
                    o = CTX + (i // 2) * P
                    ins = pe.transpose(acc[:, j * P:(j + 1) * P], xT[:, k, o:o + P], ident[:])
                end(ins)

        @block.scalar
        def _(act):
            act.wait_ge(vrow_clear, 1)
            for L in range(DEPTH):
                for at_, n, src in ((CC, 8, c_ctx), (CX, 8, c[0]), (BM, 48, b_mod[L]), (GMP, 8, g_mix_pre[L]),
                                    (GMO, 8, g_mix_post[L]), (GFP, 8, g_ffn_pre[L]), (GFO, 8, g_ffn_post[L]),
                                    (GN, 1, gla_norm[L])):
                    act.dma_start(vrow[at_:at_ + n, L, :],
                                  src.rearrange("(r p) -> r p", p=P)).then_inc(consts_in[L], 16)
                act.dma_start(vrow[BD:BD + 4, L, :],
                              b_decay[L].rearrange("d (r p) -> (d r) p", p=P)).then_inc(consts_in[L], 16)
                act.dma_start(vrow[CW:CW + 12, L, :],
                              conv_w[L].rearrange("d (r p) -> (d r) p", p=P)).then_inc(consts_in[L], 16)
                act.dma_start(wdec[:, L, :], w_decay[L].rearrange("d r n -> (d r) n")).then_inc(consts_in[L], 16)
            act.dma_start(wr[:], w_router[0].rearrange("(k p) e -> p k e", p=P)).then_inc(router_in, 16)

            n_sq = [0]
            n_rs = [0]
            steps = [0]

            def step(ins):
                steps[0] += 1
                ins.then_inc(astep, 1)
                return steps[0]

            def square(src, n):
                i = n_sq[0]
                if i >= 2:
                    act.wait_ge(*sq_free[i - 2])
                act.activation(sq[:, i % 2, 0:n], src, ACT.Square).then_inc(sq_ready, 1)
                n_sq[0] += 1

            def inverse_rms(name, n, width):
                wait_tile(act, name)
                i = n_rs[0]
                if i >= 2:
                    act.wait_ge(*rs_free[i - 2])
                r = rs[:, i % 2, 0:n]
                drains(act.activation(r, bank(name)[:, 0:n], ACT.Ln, scale=1.0 / width, bias=eps[:]), name)
                wait_drained(act, name)
                act.activation(r, r, ACT.Exp, scale=-0.5).then_inc(rs_ready, 1)
                n_rs[0] += 1

            def take_vectors(L):
                wait_tile(act, ("vec", L))
                drains(act.copy(vecs[:, L, :], bank(("vec", L))[:, 0:VROWS]), ("vec", L))

            for k in range(KD):
                wait_tile(act, ("xt", k))
                drains(act.copy(xT[:, k, :], bank(("xt", k))[:]), ("xt", k))
            take_vectors(0)
            wait_drained(act, ("vec", 0))
            act.wait_ge(consts_done, 1)
            act.activation(csil[:, :, 0], vecs[:, 0, CC:CC + 8], ACT.Silu).then_inc(csil_ready, 1)
            act.activation(csil[:, :, 1], vecs[:, 0, CX:CX + 8], ACT.Silu).then_inc(csil_ready, 1)

            def take_rows(layer, chunks):
                for i in chunks:
                    wait_tile(act, ("mrow", layer, i))
                    if (layer, i) != (0, 0):
                        wait_tile(act, ("mcol", *mod_order[mod_order.index((layer, i)) - 1]))
                    drains(act.copy(mrow, bank(("mrow", layer, i))[:]), ("mrow", layer, i))

            take_rows(0, MODS["start"])
            take_vectors(1)

            for L in range(DEPTH):
                c0 = first_col(L)
                n = TOK - c0
                v = vecs[:, L, :]
                for k in range(KD):
                    if L == 0:
                        wait_drained(act, ("xt", k))
                    else:
                        act.wait_ge(res_ready, (2 * L - 1) * KD + k + 1)
                    square(xT[:, k, :], TOK)
                inverse_rms(("ssq", 2 * L), TOK, D)
                for m in range(RT):
                    wait_tile(act, ("q", L, m))
                    drains(act.mul(qT[:, m, c0:], bank(("q", L, m))[:, 0:n], DK ** -0.5), ("q", L, m))
                for m in range(RT):
                    wait_tile(act, ("k", L, m))
                    drains(act.copy(kT[:, m, :], bank(("k", L, m))[:]), ("k", L, m))
                for i in range(4):
                    wait_tile(act, ("z", L, i))
                    drains(act.activation(la[:, i // 2, i % 2, :], bank(("z", L, i))[:], ACT.Identity,
                                          bias=v[:, BD + i:BD + i + 1]), ("z", L, i))
                e4 = lvl[:, 0].rearrange("p a r t -> p (a r) t")
                for i in range(4):
                    wait_drained(act, ("z", L, i))
                    step(act.activation(e4[:, i, :], la[:, i // 2, i % 2, :], ACT.Abs))
                act.wait_ge(astep, steps[0])
                step(act.activation(lvl[:, 0], lvl[:, 0], ACT.Exp, scale=-1.0))
                act.wait_ge(astep, steps[0])
                act.activation(lvl[:, 0], lvl[:, 0], ACT.Ln, bias=one[:]).then_inc(lnz_ready, 1)
                for g in range(NG):
                    wait_tile(act, ("v", L, g))
                    drains(act.copy(vtok[:, g, :], bank(("v", L, g))[:]), ("v", L, g))
                for s in range(len(LEVELS)):
                    for side in range(2):
                        act.wait_ge(diff_ready, 4 * (len(LEVELS) * L + s) + 2 * side + 2)
                        buf = lvl[:, s % 2, side, :, c0:]
                        act.activation(buf, buf, ACT.Exp, scale=1.0 / GATE_NORM).then_inc(decay_ready, 1)
                    if L == 0 and s < 5:
                        take_rows(0, (4 + s,))
                    if s < 2:
                        for m in (2 * s, 2 * s + 1):
                            wait_tile(act, ("g", L, m))
                            drains(act.copy(mixT[:, m, c0:], bank(("g", L, m))[:, 0:n]), ("g", L, m))
                    else:
                        wait_tile(act, ("C", L, s - 2))
                        if s > 2:
                            act.wait_ge(conv_read, 4 * L + s - 2)
                        drains(act.copy(tmp[:, 0, 0:n], bank(("C", L, s - 2))[:, 0:n]), ("C", L, s - 2))
                if L == 0:
                    take_rows(0, MODS["keys"])
                for d in range(2):
                    act.wait_ge(state_diff, 2 * L + d + 1)
                    act.activation(lvl[:, 0, d], lvl[:, 0, d], ACT.Exp, scale=1.0 / GATE_NORM).then_inc(state_exp, 1)
                wait_tile(act, ("P", L, len(LEVELS), 3))
                for d in range(2):
                    act.activation(lvl[:, 1, d, :, c0:], cum[:, d, :, c0:], ACT.Exp,
                                   scale=1.0 / GATE_NORM).then_inc(state_exp, 1)
                for d in range(2):
                    edge = CHUNK - 1 if d == 0 else 0
                    ends = cum[:, d].rearrange("p r (c t) -> p r c t", t=CHUNK)[:, :, :, edge]
                    act.activation(dec[:, d], ends, ACT.Exp, scale=1.0 / GATE_NORM).then_inc(state_exp, 1)
                for i in range(4):
                    wait_tile(act, ("kt", L, i))
                    g0 = 2 * (i % 2)
                    drains(act.copy(kdt[:, i // 2, g0:g0 + 2, :],
                                    bank(("kt", L, i))[:].rearrange("p (g n) -> p g n", g=2)), ("kt", L, i))
                if L == 0:
                    take_rows(1, MODS["added"])
                    take_rows(1, MODS["states"])
                for m in range(HEADS):
                    wait_drained(act, ("g", L, m))
                    act.activation(mixT[:, m, c0:], mixT[:, m, c0:], ACT.Silu).then_inc(gate_ready, 1)
                if L == 0:
                    take_rows(1, MODS["outputs"])
                for h in range(HEADS):
                    wait_tile(act, ("o", L, h))
                    square(bank(("o", L, h))[:, 0:n], n)
                for h in range(HEADS):
                    inverse_rms(("oss", L, h), n, DV)

                def collect(names, n, c0):
                    for m in range(KD):
                        wait_tile(act, names(m))
                        drains(act.copy(hT[:, m, c0:], bank(names(m))[:, 0:n]), names(m))
                        wait_drained(act, names(m))
                        square(hT[:, m, c0:], n)

                collect(lambda m: ("y", L, m), n, c0)
                inverse_rms(("yss", 2 * L), n, D)
                if L == 0:
                    take_rows(1, MODS["residual"])
                for k in range(KD):
                    act.wait_ge(res_ready, 2 * L * KD + k + 1)
                    square(xT[:, k, c0:], n)
                inverse_rms(("ssq", 2 * L + 1), n, D)
                if L == 0:
                    for j in range(JF):
                        wait_tile(act, ("ffg", j))
                        if j >= 2:
                            wait_drained(act, ("ffu", j - 2))
                        drains(act.activation(tmp[:, j % 2, :], bank(("ffg", j))[:], ACT.Silu), ("ffg", j))
                    collect(lambda m: ("y2", m), n, 0)
                    inverse_rms(("yss", 1), n, D)

            for i in range(4):
                wait_tile(act, ("ht", i))
                drains(act.copy(htok[:, i // 2, (i % 2) * 512:(i % 2 + 1) * 512], bank(("ht", i))[:]), ("ht", i))
            act.wait_ge(logits_in, 2)
            act.activation(small[:, 4:6, :], small[:, 2:4, :], ACT.Exp).then_inc(ex_ready, 1)
            act.sem_inc(y_drained, 1)
            act.wait_ge(route_ready, 1)

            act.sem_inc(raw_copied, 2)

            def few(e):
                H = WIDTHS[0]
                with act.Fori(0, JE // BODY) as q:
                    for j in range(BODY + 1):
                        if j < BODY:
                            act.wait_ge(raw_ready, e * JE + q * BODY + (j + 1))
                            act.copy(raw[:, j % 2, :], ps[2 + j % 2][:, 0:P]).then_inc(raw_copied, 1)
                        if j:
                            act.wait_ge(gu_ready, e * JE + q * BODY + j)
                            act.wait_ge(gu_drained, e * JE + q * BODY + j)
                            act.activation(esg[:, (j - 1) % 2, 0:H], ps[4 + (j - 1) % 2][:, 0:H],
                                           ACT.Silu).then_inc(esg_ready, 1)
                act.wait_ge(piece_free[ESLOTS - 1], e * (JE // ESLOTS) + (JE // ESLOTS + 1))
                for b in range(4):
                    act.copy(yhalf[:, b * P:(b + 1) * P], ps[0][:, b * P:(b + 1) * P]).then_inc(y_drained, 1)

            def expert(e, W):
                if W == WIDTHS[0]:
                    return few(e)
                act.sem_inc(raw_copied, JE)
                with act.Fori(0, JE // BODY) as q:
                    for j in range(BODY):
                        act.wait_ge(gu_ready, e * JE + q * BODY + (j + 1))
                        act.wait_ge(gu_drained, e * JE + q * BODY + (j + 1))
                        act.activation(esg[:, j % 2, 0:W], ps[4 + j % 2][:, 0:W], ACT.Silu).then_inc(esg_ready, 1)
                act.wait_ge(piece_free[ESLOTS - 1], e * (JE // ESLOTS) + (JE // ESLOTS + 1))
                for b in range(4):
                    act.copy(ye[:, 2 * b:2 * b + 2, 0:W],
                             ps[b][:].rearrange("p (m t) -> p m t", m=2)[:, :, 0:W]).then_inc(y_drained, 1)

            with act.Fori(0, NE) as e:
                chosen = act.value_load(cnt_i[0:1, bass.ds(e, 1)], min_val=0, max_val=SEQ)
                by_width(act, chosen, lambda W: expert(e, W))
            act.wait_ge(misc_drained, NE * MISC + 2)
            for k in range(KD):
                square(yacc[:, k, :], SEQ)
            inverse_rms(("yss", 3), SEQ, D)

        @block.vector
        def _(dve):
            steps = [0]
            n_rs = [0]

            def step(ins):
                steps[0] += 1
                ins.then_inc(vstep, 1)
                return steps[0]

            def wait_step(n=None):
                dve.wait_ge(vstep, steps[0] if n is None else n)

            step(dve.memset(eps[:], EPS))
            step(dve.memset(one[:], 1.0))
            step(dve.memset(ones[:], 1.0))
            step(dve.memset(csil[:], 0.0))
            dve.wait_ge(iota_done, 4)
            step(dve.tensor_tensor(ixor, iota_i, iota_j, ALU.bitwise_xor))
            step(dve.tensor_scalar(first0[:], iota_t, 0.5, None, ALU.is_gt))
            step(dve.tensor_scalar(last0[:], iota_t, CHUNK - 1.5, None, ALU.is_lt))
            step(dve.tensor_scalar(rank_rows[:, 0:1], iota_r, RANK - 0.5, None, ALU.is_lt))
            step(dve.tensor_scalar(rank_rows[:, 1:2], iota_r, RANK - 0.5, None, ALU.is_gt))
            wait_step()
            step(dve.tensor_scalar(ident[:], ixor, 0.0, None, ALU.is_equal))
            for s, half in enumerate(LEVELS):
                step(dve.tensor_scalar(itmp, ixor, float(2 * half), None, ALU.is_ge))
                wait_step()
                step(dve.scalar_tensor_tensor(out=masks[:, s, :], in0=ixor, scalar=float(half), in1=itmp,
                                              op0=ALU.is_ge, op1=ALU.subtract))
                wait_step()
            dve.tensor_copy(itmp, ident[:]).then_inc(consts_done, 1)

            def high_part(dst, src):
                return dve.tensor_copy(dst, src)

            def low_part(dst, src, high):
                return dve.tensor_tensor(dst, src, high, ALU.subtract)

            def split_unit(u):
                ch = ("ff", u // 4)
                dve.wait_ge(chunk_in[chunk_at[ch] % SLOTS], chunk_value[ch])
                if u >= 3:
                    wait_tile(dve, unit_tile(u - 3))
                step(high_part(w_high[:, u % 3], unit_weights(u)))
                wait_step()
                low_part(unit_weights(u, ring_r), unit_weights(u), w_high[:, u % 3].bitcast(F32)).then_inc(w_split, 1)

            def split_step(d):
                half, k = d // JF, d % JF
                ch = ("w2", half, k // 8)
                w = slot(ch).rearrange("p (k n) -> p k n", k=KD)[:, k % 8, :]
                w_low = slot(ch, ring_r).rearrange("p (k n) -> p k n", k=KD)[:, k % 8, :]
                if k == 0:
                    wait_tile(dve, unit_tile(UNITS - 1) if half == 0 else ("y2", 3))
                dve.wait_ge(chunk_in[chunk_at[ch] % SLOTS], chunk_value[ch])
                if k >= 2:
                    dve.wait_ge(w2_used, half * (JF - 1) + k - 1)
                wait_drained(dve, ("ffu", k))
                step(high_part(ff_high[:, d % 2, :], ffh[:, k, :]))
                step(high_part(w2_high[:, d % 2, :], w))
                dve.wait_ge(vstep, steps[0] - 1)
                low_part(ff_low[:, d % 2, :], ffh[:, k, :], ff_high[:, d % 2, :].bitcast(F32)).then_inc(w2_split, 1)
                wait_step()
                low_part(w_low, w, w2_high[:, d % 2, :].bitcast(F32)).then_inc(w2_split, 1)

            def by_tile(src, c0, off, done, count, each):
                n = TOK - c0
                r = rs[:, n_rs[0] % 2, 0:n]
                dve.wait_ge(rs_ready, n_rs[0] + 1)
                divided = [None] * KD

                def divide(k):
                    if k >= 2:
                        dve.wait_ge(done, count + k - 1)
                    ins = dve.tensor_tensor(tmp[:, k % 2, 0:n], src[:, k, c0 - off:], r, ALU.mult)
                    if k == KD - 1:
                        ins.then_inc(rs_used, 1)
                        divided[k] = rs_free[n_rs[0]]
                    else:
                        divided[k] = (vstep, step(ins))

                divide(0)
                for k in range(KD):
                    if k + 1 < KD:
                        divide(k + 1)
                    dve.wait_ge(*divided[k])
                    each(k, tmp[:, k % 2, 0:n])
                dve.wait_ge(done, count + KD)
                n_rs[0] += 1

            def normalise(norm, src, dst, c0, scale, shift, split=False):
                def each(k, t):
                    if c0 == 0:
                        step(dve.tensor_scalar(dst[:, k, 0:CTX], t[:, 0:CTX], scale[:, k, 0:1],
                                               shift[:, k, 0:1], ALU.mult, ALU.add))
                        wait_step()
                    dve.tensor_scalar(dst[:, k, CTX:], t[:, CTX - c0:], scale[:, k, 1:2],
                                      shift[:, k, 1:2], ALU.mult, ALU.add).then_inc(h_ready, 1)
                    if split:
                        dve.wait_ge(h_ready, KD * norm + k + 1)
                        step(high_part(x_high[:, k, :], dst[:, k, :]))
                        wait_step()
                        low_part(x_low[:, k, :], dst[:, k, :], x_high[:, k, :].bitcast(F32)).then_inc(x_split, 1)

                by_tile(src, c0, 0, h_ready, KD * norm, each)

            def add_branch(post, src, c0, gate, off=0):
                def each(k, t):
                    if c0 == 0:
                        step(dve.scalar_tensor_tensor(out=xT[:, k, 0:CTX], in0=t[:, 0:CTX],
                                                      scalar=gate[:, k, 0:1], in1=xT[:, k, 0:CTX],
                                                      op0=ALU.mult, op1=ALU.add))
                        wait_step()
                    dve.scalar_tensor_tensor(out=xT[:, k, CTX:], in0=t[:, CTX - c0:],
                                             scalar=gate[:, k, 1:2], in1=xT[:, k, CTX:],
                                             op0=ALU.mult, op1=ALU.add).then_inc(res_ready, 1)

                by_tile(src, c0, off, res_ready, KD * post, each)

            def take_mods(layer, chunks):
                for i in chunks:
                    name = ("mcol", layer, i)
                    s, k0 = i // 2, 4 * (i % 2)
                    wait_drained(dve, ("vec", layer))
                    wait_tile(dve, name)
                    part_ = bank(name)[:].rearrange("p (m g j) -> p m j g", m=4, g=4)[:, :, 0:2, :]
                    dst = modv[:, layer, s, k0:k0 + 4, :]
                    drains(dve.tensor_reduce(dst, part_, AX_X, ALU.add), name)
                    wait_drained(dve, name)
                    bias = vecs[:, layer, BM + 4 * i:BM + 4 * i + 4].unsqueeze(2).broadcast_to([P, 4, 2])
                    step(dve.tensor_tensor(dst, dst, bias, ALU.add))
                    wait_step()
                    gain = {1: GMP, 2: GMO, 4: GFP, 5: GFO}.get(s)
                    if gain is not None:
                        g = vecs[:, layer, gain + k0:gain + k0 + 4].unsqueeze(2).broadcast_to([P, 4, 2])
                        add = 1.0 if s in (1, 4) else 0.0
                        step(dve.scalar_tensor_tensor(out=dst, in0=dst, scalar=add, in1=g, op0=ALU.add, op1=ALU.mult))
                        wait_step()

            take_mods(0, MODS["start"])

            for L in range(DEPTH):
                c0 = first_col(L)
                n = TOK - c0
                v = vecs[:, L, :]
                if L == 0:
                    for k in range(KD):
                        wait_drained(dve, ("xt", k))
                normalise(2 * L, xT, hT, 0, modv[:, L, 1], modv[:, L, 0])
                wait_tile(dve, ("a", L))
                acc = bank(("a", L))
                step(dve.tensor_scalar(a2[:, 0, :], acc[0:2 * RANK, :], rank_rows[:, 0:1], None, ALU.mult))
                drains(dve.tensor_scalar(a2[:, 1, :], acc[0:2 * RANK, :], rank_rows[:, 1:2], None, ALU.mult), ("a", L))
                wait_step()
                dve.wait_ge(lnz_ready, L + 1)
                step(dve.scalar_tensor_tensor(out=la.rearrange("p d r t -> p (d r t)"),
                                              in0=la.rearrange("p d r t -> p (d r t)"), scalar=0.0,
                                              in1=lvl[:, 0].rearrange("p a r t -> p (a r t)"),
                                              op0=ALU.min, op1=ALU.subtract))
                wait_step()
                for r in range(RT):
                    step(dve.tensor_tensor_scan(cum[:, 0, r, :], first0[:], la[:, 0, r, :], 0.0, ALU.mult, ALU.add))
                    step(dve.tensor_tensor_scan(cum[:, 1, r, ::-1], last0[:, ::-1], la[:, 1, r, ::-1], 0.0,
                                                ALU.mult, ALU.add))
                wait_step()

                def halves(a, half):
                    return a.rearrange("p r (n two h) -> p r n two h", two=2, h=half)

                def differences(s):
                    half = LEVELS[s]
                    f, b = halves(cum[:, 0, :, c0:], half), halves(cum[:, 1, :, c0:], half)
                    shape = [P, RT, n // (2 * half), half]
                    left_end = f[:, :, :, 0, half - 1:half].broadcast_to(shape)
                    right_end = b[:, :, :, 1, 0:1].broadcast_to(shape)
                    q_, k_ = halves(lvl[:, s % 2, 0, :, c0:], half), halves(lvl[:, s % 2, 1, :, c0:], half)
                    if s >= 2:
                        wait_tile(dve, ("P", L, s - 1, 3))
                    for o, i0, i1 in ((q_[:, :, :, 1], f[:, :, :, 1], left_end),
                                      (q_[:, :, :, 0], b[:, :, :, 0], right_end),
                                      (k_[:, :, :, 0], left_end, f[:, :, :, 0]),
                                      (k_[:, :, :, 1], right_end, b[:, :, :, 1])):
                        dve.tensor_tensor(o, i0, i1, ALU.subtract).then_inc(diff_ready, 1)

                def take_scores(s):
                    for b in range(c0 // P, 4):
                        name = ("P", L, s, b)
                        wait_tile(dve, name)
                        acc = bank(name)[:].rearrange("p (a b) -> p a b", a=4)
                        if s == 0:
                            same = ident[:].unsqueeze(1).broadcast_to([P, 4, P])
                            drains(dve.scalar_tensor_tensor(out=att[:, b], in0=acc, scalar=2.0, in1=same,
                                                            op0=ALU.mult, op1=ALU.mult), name)
                        else:
                            wait_drained(dve, ("P", L, s - 1, b))
                            mask = masks[:, s - 1, :].unsqueeze(1).broadcast_to([P, 4, P])
                            drains(dve.copy_predicated(att[:, b], mask, acc), name)

                def conv(i):
                    dve_h, dve_b = ("h", L, i), ("B", L, i)
                    wait_drained(dve, ("C", L, i))
                    wait_tile(dve, dve_h)
                    u = tmp[:, 1, 0:n]
                    drains(dve.tensor_tensor(u, tmp[:, 0, 0:n], bank(dve_h)[:, 0:n], ALU.mult), dve_h)
                    wait_drained(dve, dve_h)
                    y = mixT[:, HEADS + i, c0:]
                    dve.tensor_scalar(y, u, v[:, CW + 4 + i:CW + 5 + i], None, ALU.mult).then_inc(conv_read, 1)
                    dve.wait_ge(conv_read, 4 * L + i + 1)
                    for tap, dst0, src0 in ((0, 1, 0), (2, 0, 1)):
                        if L == 0:
                            ins = dve.scalar_tensor_tensor(
                                out=y[:, dst0:dst0 + CTX - 1], in0=u[:, src0:src0 + CTX - 1],
                                scalar=v[:, CW + 4 * tap + i:CW + 4 * tap + i + 1],
                                in1=y[:, dst0:dst0 + CTX - 1], op0=ALU.mult, op1=ALU.add)
                            step(ins)
                        us = u[:, CTX - c0:].rearrange("p (s t) -> p s t", t=64)
                        ys = y[:, CTX - c0:].rearrange("p (s t) -> p s t", t=64)
                        step(dve.scalar_tensor_tensor(
                            out=ys[:, :, dst0:dst0 + 63], in0=us[:, :, src0:src0 + 63],
                            scalar=v[:, CW + 4 * tap + i:CW + 4 * tap + i + 1],
                            in1=ys[:, :, dst0:dst0 + 63], op0=ALU.mult, op1=ALU.add))
                        wait_step()
                    wait_tile(dve, dve_b)
                    drains(dve.tensor_tensor(y, y, bank(dve_b)[:, 0:n], ALU.mult), dve_b)

                for m in range(RT):
                    wait_drained(dve, ("q", L, m))
                    wait_drained(dve, ("k", L, m))
                differences(0)
                take_scores(0)
                for s in range(len(LEVELS)):
                    if s + 1 < len(LEVELS):
                        differences(s + 1)
                    for side, t in ((0, qT), (1, kT)):
                        dve.wait_ge(decay_ready, 2 * (len(LEVELS) * L + s) + side + 1)
                        buf = lvl[:, s % 2, side, :, c0:]
                        dve.tensor_tensor(buf, buf, t[:, :, c0:], ALU.mult).then_inc(level_ready, 1)
                    if s > 0:
                        take_scores(s)
                    if s > 2:
                        conv(s - 3)
                    if L == 0 and s < 5:
                        take_mods(0, (4 + s,))
                conv(3)
                wait_tile(dve, ("P", L, len(LEVELS) - 1, 3))
                for d, edge in ((0, CHUNK - 1), (1, 0)):
                    b = cum[:, d].rearrange("p r (c t) -> p r c t", t=CHUNK)
                    dve.tensor_tensor(lvl[:, 0, d].rearrange("p r (c t) -> p r c t", t=CHUNK),
                                      b[:, :, :, edge:edge + 1].broadcast_to([P, RT, NCH, CHUNK]), b,
                                      ALU.subtract).then_inc(state_diff, 1)
                for d in range(2):
                    dve.wait_ge(state_exp, 6 * L + d + 1)
                    dve.tensor_tensor(lvl[:, 0, d], lvl[:, 0, d], kT, ALU.mult).then_inc(state_ops, 1)
                take_scores(len(LEVELS))
                for d in range(2):
                    dve.wait_ge(state_exp, 6 * L + d + 3)
                    dve.tensor_tensor(lvl[:, 1, d, :, c0:], lvl[:, 1, d, :, c0:], qT[:, :, c0:],
                                      ALU.mult).then_inc(state_ops, 1)
                if L == 0:
                    take_mods(0, MODS["keys"])
                    take_mods(1, MODS["added"])
                dve.wait_ge(state_exp, 6 * L + 6)
                for d in range(2):
                    order = list(range(NCH)) if d == 0 else list(range(3, -1, -1)) + list(range(NCH - 1, 3, -1))
                    seen = set()
                    for at_, ch in enumerate(order):
                        i = 2 * (ch // 4) + ch % 2
                        j = (ch % 4) // 2
                        name = ("U", L, d, i)
                        wait_tile(dve, name)
                        acc = bank(name)
                        nxt = order[at_ + 1] if at_ + 1 < NCH else None
                        closes = name in seen
                        seen.add(name)
                        for r in range(RT):
                            add = acc[:, (2 * j + r) * DV:(2 * j + r + 1) * DV]
                            if nxt is None:
                                if r == RT - 1:
                                    ins = dve.tensor_copy(small[:, 14, 0:1], acc[:, 0:1])
                                else:
                                    continue
                            elif at_ == 0:
                                ins = dve.tensor_copy(states[:, d, nxt, r, :], add)
                            else:
                                ins = dve.scalar_tensor_tensor(out=states[:, d, nxt, r, :], in0=states[:, d, ch, r, :],
                                                               scalar=dec[:, d, r, ch:ch + 1], in1=add,
                                                               op0=ALU.mult, op1=ALU.add)
                            if closes and r == RT - 1:
                                drains(ins, name)
                                wait_drained(dve, name)
                            else:
                                step(ins)
                        wait_step()
                dve.tensor_copy(small[:, 14, 1:2], ones[:, 0:1]).then_inc(states_ready, 1)
                if L == 0:
                    take_mods(1, MODS["states"])
                    take_mods(1, MODS["outputs"])
                for h in range(HEADS):
                    r = rs[:, n_rs[0] % 2, 0:n]
                    dve.wait_ge(rs_ready, n_rs[0] + 1)
                    t = tmp[:, h % 2, 0:n]
                    name = ("o", L, h)
                    wait_tile(dve, name)
                    drains(dve.tensor_tensor(t, r, bank(name)[:, 0:n], ALU.mult), name)
                    wait_drained(dve, name)
                    dve.wait_ge(gate_ready, HEADS * L + h + 1)
                    dve.scalar_tensor_tensor(out=mixT[:, h, c0:], in0=t, scalar=v[:, GN:GN + 1], in1=mixT[:, h, c0:],
                                             op0=ALU.mult, op1=ALU.mult).then_inc(mix_ready, 1)
                    n_rs[0] += 1
                add_branch(2 * L, hT, c0, modv[:, L, 2])
                if L == 0:
                    take_mods(1, MODS["residual"])
                if L == 0:
                    split_unit(0)
                    split_unit(1)
                normalise(2 * L + 1, xT, hT, c0, modv[:, L, 4], modv[:, L, 3], split=(L == 0))
                if L == 0:
                    for j in range(JF):
                        if j < JF - 1:
                            split_unit(2 * j + 2)
                            split_unit(2 * j + 3)
                        wait_tile(dve, ("ffu", j))
                        wait_drained(dve, ("ffg", j))
                        drains(dve.tensor_tensor(ffh[:, j, :], tmp[:, j % 2, :], bank(("ffu", j))[:], ALU.mult),
                               ("ffu", j))
                    for d in range(2 * JF):
                        split_step(d)
                    add_branch(1, hT, 0, modv[:, 0, 5])

            dve.wait_ge(iota2_done, 3)
            dve.tensor_copy(slotno, iota_s).then_inc(consts2_done, 1)
            dve.tensor_scalar(before, iota_b, 0.5, None, ALU.is_gt).then_inc(consts2_done, 1)
            dve.tensor_scalar(tie, iota_e, 0.5, None, ALU.is_gt).then_inc(consts2_done, 1)
            step(dve.memset(zeros, 0.0))
            dve.wait_ge(consts2_done, 3)
            wait_tile(dve, ("lg",))
            lg = small[:, 12:14, :]
            drains(dve.tensor_copy(lg, bank(("lg",))[:, 0:TT * NE].rearrange("p (t e) -> p t e", t=TT)), ("lg",))
            wait_drained(dve, ("lg",))
            top = small[:, 11, 0:TT]
            step(dve.tensor_reduce(top, lg, AX_X, ALU.max))
            wait_step()
            dve.tensor_scalar(small[:, 2, :], lg[:, 0, :], top[:, 0:1], None, ALU.subtract).then_inc(logits_in, 1)
            dve.tensor_scalar(small[:, 3, :], lg[:, 1, :], top[:, 1:2], None, ALU.subtract).then_inc(logits_in, 1)
            sel = small[:, 0:2, :]
            tie3 = tie.rearrange("p (e j) -> p e j", e=NE)
            for t in range(TT):
                mine = lg[:, t, :].unsqueeze(2).broadcast_to([P, NE, NE])
                other = lg[:, t, :].unsqueeze(1).broadcast_to([P, NE, NE])
                larger = route[:, 0, 0:NE * NE].rearrange("p (e j) -> p e j", e=NE)
                equal = route[:, 1, 0:NE * NE].rearrange("p (e j) -> p e j", e=NE)
                step(dve.tensor_tensor(larger, other, mine, ALU.is_gt))
                step(dve.tensor_tensor(equal, other, mine, ALU.is_equal))
                wait_step()
                step(dve.tensor_tensor(equal, equal, tie3, ALU.mult))
                wait_step()
                step(dve.tensor_tensor(larger, larger, equal, ALU.add))
                wait_step()
                step(dve.tensor_reduce(small[:, 10, :], larger, AX_X, ALU.add))
                wait_step()
                ins = dve.tensor_scalar(sel[:, t, :], small[:, 10, :], 1.5, None, ALU.is_lt)
                if t == TT - 1:
                    ins.then_inc(sel_counted, 1)
                    dve.wait_ge(sel_counted, 1)
                else:
                    step(ins)
                    wait_step()
            share = small[:, 6:8, :]
            dve.wait_ge(ex_ready, 1)
            step(dve.tensor_tensor(share, small[:, 4:6, :], sel, ALU.mult))
            wait_step()
            total = small[:, 11, 2:2 + TT]
            step(dve.tensor_reduce(total, share, AX_X, ALU.add))
            wait_step()
            step(dve.reciprocal(total, total))
            wait_step()
            for t in range(TT):
                step(dve.tensor_scalar(share[:, t, :], share[:, t, :], total[:, t:t + 1], None, ALU.mult))
            place = small[:, 8:10, :]
            wait_tile(dve, ("pos",))
            acc = bank(("pos",))
            step(dve.scalar_tensor_tensor(out=place, in0=acc[:, 0:TT * NE].rearrange("p (t e) -> p t e", t=TT),
                                          scalar=1.0, in1=sel, op0=ALU.add, op1=ALU.mult))
            drains(dve.tensor_copy(cnt_i[:], acc[0:1, 2 * NE:3 * NE]), ("pos",))
            wait_step()
            step(dve.tensor_scalar(place, place, 1.0, None, ALU.subtract))
            step(dve.memset(yacc, 0.0))
            step(dve.memset(ye, 0.0))
            wait_step()
            wait_drained(dve, ("pos",))
            dve.tensor_copy(small[:, 14, 2:3], ones[:, 0:1]).then_inc(route_ready, 1)
            dve.sem_inc(misc_drained, 2)
            dve.sem_inc(gu_drained, 2)

            def expert(e, W):
                few = W == WIDTHS[0]
                H = WIDTHS[0]
                u0 = H if few else 256
                sh_n = (W + P - 1) // P
                wp = min(W, P)

                def misc(i):
                    dve.wait_ge(misc_ready, e * MISC + (i + 1))
                    return ps[6 + i % 2]

                for i in range(4):
                    acc = misc(i)
                    dve.tensor_copy(xsel[:, 2 * i:2 * i + 2, 0:W],
                                    acc[:].rearrange("p (m t) -> p m t", m=2)[:, :, 0:W]).then_inc(misc_drained, 1)
                for t in range(TT):
                    acc = misc(4 + t)
                    if few:
                        dve.tensor_copy(swt[H:2 * H, 0, t * P:(t + 1) * P], acc[0:H, 0:P])
                    dve.tensor_copy(swt[0:wp, 0:sh_n, t * P:(t + 1) * P],
                                    acc[0:wp, 0:sh_n * P].rearrange("p (s t) -> p s t", s=sh_n),
                                    ).then_inc(misc_drained, 1)
                with dve.Fori(0, JE // BODY) as q:
                    for j in range(BODY):
                        dve.wait_ge(esg_ready, e * JE + q * BODY + (j + 1))
                        dve.tensor_tensor(eh[:, j % 2, 0:W], esg[:, j % 2, 0:W], ps[4 + j % 2][:, u0:u0 + W],
                                          ALU.mult).then_inc(gu_drained, 1)
                if few:
                    dve.wait_ge(misc_ready, e * MISC + 10)
                    dve.sem_inc(misc_drained, 4)
                for i in range(0 if few else 4):
                    acc = misc(6 + i)
                    dve.tensor_copy(yslot[0:wp, 0:sh_n, 2 * i * P:(2 * i + 2) * P],
                                    acc[0:wp, 0:sh_n * 256].rearrange("p (s t) -> p s t", s=sh_n),
                                    ).then_inc(misc_drained, 1)
                for i in range(4):
                    acc = misc(10 + i)
                    dve.wait_ge(misc_drained, e * MISC + (10 + i + 2))
                    dve.tensor_tensor(yacc[:, 2 * i:2 * i + 2, :], yacc[:, 2 * i:2 * i + 2, :],
                                      acc[:].rearrange("p (m t) -> p m t", m=2), ALU.add).then_inc(misc_drained, 1)

            with dve.Fori(0, NE) as e:
                for t in range(TT):
                    one_hot = place[:, t, bass.ds(e, 1)]
                    dve.tensor_scalar(selg[:, t, :], slotno, one_hot, None, ALU.is_equal).then_inc(sel_ready, 1)
                    dve.tensor_scalar(selw[:, t, :], slotno, one_hot, share[:, t, bass.ds(e, 1)],
                                      ALU.is_equal, ALU.mult).then_inc(sel_ready, 1)
                chosen = dve.value_load(cnt_i[0:1, bass.ds(e, 1)], min_val=0, max_val=SEQ)
                by_width(dve, chosen, lambda W: expert(e, W))
            add_branch(3, yacc, CTX, modv[:, 1, 5], off=CTX)
            for i in range(4):
                wait_tile(dve, ("out", i))
                drains(dve.tensor_copy(osb[:, i // 2, (i % 2) * 512:(i % 2 + 1) * 512], bank(("out", i))[:]),
                       ("out", i))


_INS = ["x", "c", "ctx", "c_ctx", "w_mod", "b_mod", "g_mix_pre", "g_mix_post", "w_in", "w_decay", "b_decay",
        "gla_norm", "conv_w", "w_out", "g_ffn_pre", "g_ffn_post", "w1", "w3", "w2", "w_router",
        "e_w1", "e_w3", "e_w2"]


def kernel(**inputs):
    import concourse.bacc as bacc
    from concourse.bass_utils import run_bass_kernel_spmd

    nc = bacc.Bacc("TRN2", target_bir_lowering=False, num_devices=1)
    arrays, args = {}, []
    for name in _INS:
        a = np.ascontiguousarray(inputs[name])
        arrays[f"in_{name}"] = a
        args.append(nc.dram_tensor(f"in_{name}", a.shape, mybir.dt.from_np(a.dtype), kind="ExternalInput").ap())
    args.append(nc.dram_tensor("out_0", (1, SEQ, D), F32, kind="ExternalOutput").ap())
    hybrid_backbone(nc, *args)
    r = run_bass_kernel_spmd(nc, [arrays], core_ids=[0])
    return r.results[0]["out_0"]
```
